# Optimizing a Trainium2 kernel written in Bass

```python
import jax, jax.numpy as jnp
from jax import lax
import numpy as np

D_MODEL = 1024
BATCH = 1
SEQ = 1024
DEPTH = 1

GRID_W = 64
N_ATT_HEADS = 8
ATT_HEAD_DIM = 64
D_ATT = N_ATT_HEADS * ATT_HEAD_DIM
WIN_H_MAX = 8
WIN_W = 16
Q_BLOCK_W = 16
KV_BLOCK_W = Q_BLOCK_W + WIN_W
N_COL_BLOCKS = GRID_W // Q_BLOCK_W
D_REC = D_MODEL
N_REC_BLOCKS = 16
REC_BLOCK = D_REC // N_REC_BLOCKS
CONV_W = 4
LRU_C = 8.0
N_DIR = 2
D_FF = 4 * D_MODEL
EPS = 1e-6
D_IN = 3 * D_ATT + 2 * D_REC + 2 * D_MODEL
SPLITS = [int(v) for v in np.cumsum([D_ATT, D_ATT, D_ATT, D_REC, D_REC, D_MODEL])]


def rms_norm(x, g):
    x32 = x.astype(jnp.float32)
    y = x32 * lax.rsqrt(jnp.mean(x32 * x32, axis=-1, keepdims=True) + EPS)
    return (y * g.astype(jnp.float32)).astype(x.dtype)

def neighbourhood_attention(q, k, v, rpb):
    b, s, h, dh = q.shape
    rows = s // GRID_W
    kh = min(WIN_H_MAX, rows)
    r = np.arange(rows)
    row_start = np.clip(r - kh // 2, 0, rows - kh)
    row_idx = row_start[:, None] + np.arange(kh)[None, :]
    n = np.arange(N_COL_BLOCKS)
    col_start = np.clip(n * Q_BLOCK_W - WIN_W // 2, 0, GRID_W - KV_BLOCK_W)
    col_idx = col_start[:, None] + np.arange(KV_BLOCK_W)[None, :]
    qc = n[:, None] * Q_BLOCK_W + np.arange(Q_BLOCK_W)[None, :]
    win_start = np.clip(qc - WIN_W // 2, 0, GRID_W - WIN_W)
    kc = col_idx[:, None, :]
    valid = (kc >= win_start[..., None]) & (kc < win_start[..., None] + WIN_W)
    d_row = row_idx - r[:, None] + (WIN_H_MAX - 1)
    d_col = np.clip(kc - qc[..., None], -(WIN_W - 1), WIN_W - 1) + (WIN_W - 1)

    scale = ATT_HEAD_DIM ** -0.5
    q_blk = (q * scale).reshape(b, rows, N_COL_BLOCKS, Q_BLOCK_W, h, dh).transpose(0, 4, 1, 2, 3, 5)
    k_grid = k.reshape(b, rows, GRID_W, h, dh).transpose(0, 3, 1, 2, 4)
    v_grid = v.reshape(b, rows, GRID_W, h, dh).transpose(0, 3, 1, 2, 4)
    ri = row_idx[:, None, :, None]
    ci = col_idx[None, :, None, :]
    kg = k_grid[:, :, ri, ci]
    vg = v_grid[:, :, ri, ci]

    scores = jnp.einsum('bhrnqd,bhrnikd->bhrnqik', q_blk, kg).astype(jnp.float32)
    bias = rpb.astype(jnp.float32)[:, d_row[:, None, None, :, None], d_col[None, :, :, None, :]]
    scores = scores + bias[None]
    scores = jnp.where(valid[:, :, None, :], scores, -1e30)
    probs = jax.nn.softmax(scores, axis=(-2, -1)).astype(v.dtype)
    out = jnp.einsum('bhrnqik,bhrnikd->bhrnqd', probs, vg)
    return out.transpose(0, 2, 3, 4, 1, 5).reshape(b, s, h * dh)

def centred_depthwise_conv(u, w, bias):
    s = u.shape[1]
    left = CONV_W // 2
    right = CONV_W - 1 - left
    up = jnp.pad(u, ((0, 0), (left, right), (0, 0)))
    out = bias
    for j in range(CONV_W):
        out = out + up[:, j:j + s] * w[j]
    return out

def block_diag_linear(u, w, b):
    bsz, s, c = u.shape
    ub = u.reshape(bsz, s, N_REC_BLOCKS, REC_BLOCK)
    return jnp.einsum('bsnc,ncd->bsnd', ub, w).reshape(bsz, s, c) + b

def rg_lru(u, w_a, b_a, w_i, b_i, lam, reverse):
    r_gate = jax.nn.sigmoid(block_diag_linear(u, w_a, b_a)).astype(jnp.float32)
    i_gate = jax.nn.sigmoid(block_diag_linear(u, w_i, b_i))
    log_a = -LRU_C * r_gate * jax.nn.softplus(-lam.astype(jnp.float32))
    a = jnp.exp(log_a)
    mult = jnp.sqrt(jnp.maximum(-jnp.expm1(2.0 * log_a), 0.0))
    bx = mult * (i_gate * u).astype(jnp.float32)

    def combine(c1, c2):
        a1, b1 = c1
        a2, b2 = c2
        return a1 * a2, a2 * b1 + b2

    _, h = lax.associative_scan(combine, (a, bx), axis=1, reverse=reverse)
    return h.astype(u.dtype)

def first_inputs(seed: int = 0) -> dict:
    key = jax.random.key(seed)
    ks = jax.random.split(key, 20)
    f32 = jnp.float32
    nrm = lambda k, shape, fan_in: jax.random.normal(k, shape, f32) * (fan_in ** -0.5)
    x = jax.random.normal(ks[0], (BATCH, SEQ, D_MODEL), f32)
    ln1_g = 1.0 + 0.05 * jax.random.normal(ks[1], (DEPTH, D_MODEL), f32)
    w_in = nrm(ks[2], (DEPTH, D_MODEL, D_IN), D_MODEL)
    b_in = 0.02 * jax.random.normal(ks[3], (DEPTH, D_IN), f32)
    rpb = 0.02 * jax.random.normal(ks[4], (DEPTH, N_ATT_HEADS, 2 * WIN_H_MAX - 1, 2 * WIN_W - 1), f32)
    w_att_o = nrm(ks[5], (DEPTH, D_ATT, D_MODEL), D_ATT)
    conv_w = nrm(ks[6], (DEPTH, CONV_W, D_REC), CONV_W)
    conv_b = 0.02 * jax.random.normal(ks[7], (DEPTH, D_REC), f32)
    w_rg_a = nrm(ks[8], (DEPTH, N_DIR, N_REC_BLOCKS, REC_BLOCK, REC_BLOCK), REC_BLOCK)
    b_rg_a = 0.02 * jax.random.normal(ks[9], (DEPTH, N_DIR, D_REC), f32)
    w_rg_i = nrm(ks[10], (DEPTH, N_DIR, N_REC_BLOCKS, REC_BLOCK, REC_BLOCK), REC_BLOCK)
    b_rg_i = 0.02 * jax.random.normal(ks[11], (DEPTH, N_DIR, D_REC), f32)
    a_c = jax.random.uniform(ks[12], (DEPTH, N_DIR, D_REC), f32, 0.9, 0.999)
    a0 = a_c ** (1.0 / LRU_C)
    lru_lambda = jnp.log(a0) - jnp.log1p(-a0)
    w_rec_o = nrm(ks[13], (DEPTH, D_REC, D_MODEL), D_REC)
    w_out = nrm(ks[14], (DEPTH, D_MODEL, D_MODEL), D_MODEL)
    ln2_g = 1.0 + 0.05 * jax.random.normal(ks[15], (DEPTH, D_MODEL), f32)
    w_ff1 = nrm(ks[16], (DEPTH, D_MODEL, D_FF), D_MODEL)
    w_ff2 = nrm(ks[17], (DEPTH, D_FF, D_MODEL), D_FF)
    lnf_g = 1.0 + 0.05 * jax.random.normal(ks[18], (D_MODEL,), f32)
    return {"x": x, "ln1_g": ln1_g, "w_in": w_in, "b_in": b_in, "rpb": rpb,
            "w_att_o": w_att_o, "conv_w": conv_w, "conv_b": conv_b,
            "w_rg_a": w_rg_a, "b_rg_a": b_rg_a, "w_rg_i": w_rg_i, "b_rg_i": b_rg_i,
            "lru_lambda": lru_lambda, "w_rec_o": w_rec_o, "w_out": w_out,
            "ln2_g": ln2_g, "w_ff1": w_ff1, "w_ff2": w_ff2, "lnf_g": lnf_g}

def first_block(x, ln1_g, w_in, b_in, rpb, w_att_o, conv_w, conv_b, w_rg_a, b_rg_a,
              w_rg_i, b_rg_i, lru_lambda, w_rec_o, w_out, ln2_g, w_ff1, w_ff2, lnf_g):
    b, s, _ = x.shape
    for l in range(DEPTH):
        h = rms_norm(x, ln1_g[l])
        z = h @ w_in[l] + b_in[l]
        q, k, v, u, y_branch, g_att, g_rec = jnp.split(z, SPLITS, axis=-1)

        q = q.reshape(b, s, N_ATT_HEADS, ATT_HEAD_DIM)
        k = k.reshape(b, s, N_ATT_HEADS, ATT_HEAD_DIM)
        v = v.reshape(b, s, N_ATT_HEADS, ATT_HEAD_DIM)
        y_att = neighbourhood_attention(q, k, v, rpb[l]) @ w_att_o[l]

        u = centred_depthwise_conv(u, conv_w[l], conv_b[l])
        h_fwd = rg_lru(u, w_rg_a[l, 0], b_rg_a[l, 0], w_rg_i[l, 0], b_rg_i[l, 0], lru_lambda[l, 0], False)
        h_bwd = rg_lru(u, w_rg_a[l, 1], b_rg_a[l, 1], w_rg_i[l, 1], b_rg_i[l, 1], lru_lambda[l, 1], True)
        y_rec = ((h_fwd + h_bwd) * jax.nn.gelu(y_branch)) @ w_rec_o[l]

        mixed = jax.nn.sigmoid(g_att) * y_att + jax.nn.sigmoid(g_rec) * y_rec
        x = x + mixed @ w_out[l]

        h2 = rms_norm(x, ln2_g[l])
        x = x + jnp.square(jax.nn.relu(h2 @ w_ff1[l])) @ w_ff2[l]
    return rms_norm(x, lnf_g)


CTX_LEN = 256
HEAD_DIM = 64
ATTN_Q_HEADS = 8
ATTN_KV_HEADS = 2
ATTN_GROUP = ATTN_Q_HEADS // ATTN_KV_HEADS
WINDOW = 128
ATTN_BLOCK = 128
ROPE_BASE = 10000.0
DN_HEADS = 8
DN_HEAD_DIM = 64
CONV_W_2 = 3
CHUNK = 64
D_FF_2 = 4 * D_MODEL
NEG_INF = -1e30

ATTN_WIDTH = ATTN_Q_HEADS * HEAD_DIM
KV_WIDTH = ATTN_KV_HEADS * HEAD_DIM
DN_WIDTH = DN_HEADS * DN_HEAD_DIM
IN_SPLITS = (ATTN_WIDTH, KV_WIDTH, KV_WIDTH, DN_WIDTH, DN_WIDTH, DN_WIDTH, DN_WIDTH,
             N_DIR * DN_HEADS, N_DIR * DN_HEADS, D_MODEL, D_MODEL)
IN_WIDTH = 4 * DN_WIDTH + ATTN_WIDTH + 2 * KV_WIDTH + 2 * N_DIR * DN_HEADS + 2 * D_MODEL


def rms_norm_2(x, g):
    xf = x.astype(jnp.float32)
    return xf * lax.rsqrt(jnp.mean(xf * xf, axis=-1, keepdims=True) + EPS) * g.astype(jnp.float32)

def l2_normalize(x):
    return x * lax.rsqrt(jnp.sum(x * x, axis=-1, keepdims=True) + EPS)

def split_cols(p):
    offsets = [int(o) for o in np.cumsum(IN_SPLITS)[:-1]]
    return jnp.split(p, offsets, axis=-1)

def axial_rope(x, row, col):
    half = HEAD_DIM // 2
    n_freq = half // 2
    freqs = ROPE_BASE ** (-jnp.arange(n_freq, dtype=jnp.float32) / n_freq)

    def rot(xh, pos):
        ang = pos.astype(jnp.float32)[:, None] * freqs
        cos = jnp.cos(ang)[None, :, None, :]
        sin = jnp.sin(ang)[None, :, None, :]
        x1, x2 = xh[..., :n_freq], xh[..., n_freq:]
        return jnp.concatenate([x1 * cos - x2 * sin, x1 * sin + x2 * cos], axis=-1)

    return jnp.concatenate([rot(x[..., :half], row), rot(x[..., half:], col)], axis=-1)

def centred_short_conv(x, w):
    pad = CONV_W_2 // 2
    T = x.shape[1]
    xp = jnp.pad(x, ((0, 0), (pad, CONV_W_2 - 1 - pad), (0, 0)))
    y = sum(xp[:, tap:tap + T] * w[tap] for tap in range(CONV_W_2))
    return jax.nn.silu(y)

def gated_delta_chunked(q, k, v, g_log, beta, s0):
    B, T, H, dk = q.shape
    n = T // CHUNK

    def chunks(a):
        return jnp.moveaxis(a.reshape((B, n, CHUNK, H) + a.shape[3:]), 3, 1)

    qc, kc, vc = chunks(q), chunks(k), chunks(v)
    gc, bc = chunks(g_log), chunks(beta)
    G = jnp.cumsum(gc, axis=-1)
    idx = jnp.arange(CHUNK)
    strict = idx[:, None] > idx[None, :]
    incl = idx[:, None] >= idx[None, :]
    diff = G[..., :, None] - G[..., None, :]
    dec_strict = jnp.where(strict, jnp.exp(jnp.where(strict, diff, 0.0)), 0.0)
    dec_incl = jnp.where(incl, jnp.exp(jnp.where(incl, diff, 0.0)), 0.0)
    kk = jnp.einsum('bhnid,bhnjd->bhnij', kc, kc)
    t_mat = jnp.eye(CHUNK, dtype=jnp.float32) + bc[..., :, None] * dec_strict * kk
    eG = jnp.exp(G)
    w_mat = lax.linalg.triangular_solve(t_mat, (bc * eG)[..., None] * kc, left_side=True, lower=True,
                                        unit_diagonal=True)
    u_v = lax.linalg.triangular_solve(t_mat, bc[..., None] * vc, left_side=True, lower=True,
                                      unit_diagonal=True)
    intra = dec_incl * jnp.einsum('bhnid,bhnjd->bhnij', qc, kc)
    q_dec = eG[..., None] * qc
    g_last = G[..., -1]
    k_tail = jnp.exp(g_last[..., None] - G)[..., None] * kc

    def step(S, xs):
        w_c, uv_c, qd_c, intra_c, kt_c, gl_c = xs
        u = uv_c - jnp.einsum('bhck,bhkv->bhcv', w_c, S)
        o = jnp.einsum('bhck,bhkv->bhcv', qd_c, S) + jnp.einsum('bhij,bhjv->bhiv', intra_c, u)
        S = jnp.exp(gl_c)[..., None, None] * S + jnp.einsum('bhck,bhcv->bhkv', kt_c, u)
        return S, o

    xs = tuple(jnp.moveaxis(a, 2, 0) for a in (w_mat, u_v, q_dec, intra, k_tail, g_last))
    s_final, o = lax.scan(step, s0, xs)
    o = jnp.transpose(o, (1, 0, 3, 2, 4)).reshape(B, T, H, v.shape[-1])
    return o, s_final

def bidir_delta(q, k, v, g, beta, s0_f, s0_b):
    o_f, s_f = gated_delta_chunked(q, k, v, g[:, :, 0], beta[:, :, 0], s0_f)
    flip = lambda a: jnp.flip(a, axis=1)
    o_b, s_b = gated_delta_chunked(flip(q), flip(k), flip(v), flip(g[:, :, 1]), flip(beta[:, :, 1]), s0_b)
    return o_f + flip(o_b), s_f, s_b

def window_ctx_attention(q, k, v, k_ctx, v_ctx, sink):
    B, S = q.shape[:2]
    L = k_ctx.shape[1]
    nb = S // ATTN_BLOCK
    qb = q.reshape(B, nb, ATTN_BLOCK, ATTN_KV_HEADS, ATTN_GROUP, HEAD_DIM)

    def band(a):
        ap = jnp.pad(a, ((0, 0), (ATTN_BLOCK, ATTN_BLOCK), (0, 0), (0, 0)))
        ap = ap.reshape(B, nb + 2, ATTN_BLOCK, ATTN_KV_HEADS, HEAD_DIM)
        return jnp.concatenate([ap[:, :-2], ap[:, 1:-1], ap[:, 2:]], axis=2)

    kb, vb = band(k), band(v)
    blk = jnp.arange(nb)[:, None, None]
    qpos = blk * ATTN_BLOCK + jnp.arange(ATTN_BLOCK)[None, :, None]
    kpos = (blk - 1) * ATTN_BLOCK + jnp.arange(3 * ATTN_BLOCK)[None, None, :]
    valid = (jnp.abs(qpos - kpos) <= WINDOW) & (kpos >= 0) & (kpos < S)
    scale = HEAD_DIM ** -0.5
    s_loc = jnp.einsum('bnqgrd,bnkgd->bngrqk', qb, kb) * scale
    s_loc = jnp.where(valid[None, :, None, None], s_loc, NEG_INF)
    s_ctx = jnp.einsum('bnqgrd,bkgd->bngrqk', qb, k_ctx) * scale
    s_sink = jnp.broadcast_to(sink.reshape(ATTN_KV_HEADS, ATTN_GROUP)[None, None, :, :, None, None],
                              s_loc.shape[:-1] + (1,))
    p = jax.nn.softmax(jnp.concatenate([s_loc, s_ctx, s_sink], axis=-1).astype(jnp.float32), axis=-1)
    n_loc = 3 * ATTN_BLOCK
    o = (jnp.einsum('bngrqk,bnkgd->bnqgrd', p[..., :n_loc], vb)
         + jnp.einsum('bngrqk,bkgd->bnqgrd', p[..., n_loc:n_loc + L], v_ctx))
    return o.reshape(B, S, ATTN_WIDTH)

def ctx_self_attention(q, k, v, sink):
    B, L = q.shape[:2]
    qg = q.reshape(B, L, ATTN_KV_HEADS, ATTN_GROUP, HEAD_DIM)
    s = jnp.einsum('bqgrd,bkgd->bgrqk', qg, k) * HEAD_DIM ** -0.5
    s_sink = jnp.broadcast_to(sink.reshape(ATTN_KV_HEADS, ATTN_GROUP)[None, :, :, None, None], s.shape[:-1] + (1,))
    p = jax.nn.softmax(jnp.concatenate([s, s_sink], axis=-1).astype(jnp.float32), axis=-1)
    o = jnp.einsum('bgrqk,bkgd->bqgrd', p[..., :L], v)
    return o.reshape(B, L, ATTN_WIDTH)

def trunk_layer(x, ctx, c, c_ctx, w_ada, b_ada, g_norm1, w_in, q_norm_g, k_norm_g, attn_sink, conv_w,
                a_log, dt_bias, dn_norm_g, w_br_attn, w_br_dn, w_out, g_norm2, w_mlp1, w_mlp2, update_ctx):
    B, S = x.shape[:2]
    L = ctx.shape[1]
    rows = S // GRID_W
    row = jnp.broadcast_to(jnp.arange(rows)[:, None], (rows, GRID_W)).reshape(-1)
    col = jnp.broadcast_to(jnp.arange(GRID_W)[None, :], (rows, GRID_W)).reshape(-1)

    mod = jax.nn.silu(c.astype(jnp.float32)) @ w_ada + b_ada
    mod_c = jax.nn.silu(c_ctx.astype(jnp.float32)) @ w_ada + b_ada
    sh1, sc1, gt1, sh2, sc2, gt2 = [m[:, None] for m in jnp.split(mod, 6, axis=-1)]
    csh1, csc1, cgt1, csh2, csc2, cgt2 = jnp.split(mod_c, 6, axis=-1)

    h = rms_norm_2(x, g_norm1) * (1.0 + sc1) + sh1
    hc = rms_norm_2(ctx, g_norm1) * (1.0 + csc1) + csh1
    aq, ak, av, dq, dk, dv, dz, da, db, ga, gd = split_cols(h @ w_in)
    caq, cak, cav, cdq, cdk, cdv, cdz, cda, cdb, cga, cgd = split_cols(hc @ w_in)

    def heads(a, n_heads):
        return a.reshape(a.shape[0], a.shape[1], n_heads, HEAD_DIM)

    q_a = axial_rope(rms_norm_2(heads(aq, ATTN_Q_HEADS), q_norm_g), row, col)
    k_a = axial_rope(rms_norm_2(heads(ak, ATTN_KV_HEADS), k_norm_g), row, col)
    v_a = heads(av, ATTN_KV_HEADS)
    k_ac = rms_norm_2(heads(cak, ATTN_KV_HEADS), k_norm_g)
    v_ac = heads(cav, ATTN_KV_HEADS)
    y_attn = window_ctx_attention(q_a, k_a, v_a, k_ac, v_ac, attn_sink)

    def dn_inputs(pq, pk, pv, pa, pb):
        qkv = centred_short_conv(jnp.concatenate([pq, pk, pv], axis=-1), conv_w)
        q_d, k_d, v_d = jnp.split(qkv, 3, axis=-1)
        q_d = l2_normalize(heads(q_d, DN_HEADS)) * DN_HEAD_DIM ** -0.5
        k_d = l2_normalize(heads(k_d, DN_HEADS))
        v_d = heads(v_d, DN_HEADS)
        T = pq.shape[1]
        beta = jax.nn.sigmoid(pb.reshape(pb.shape[0], T, N_DIR, DN_HEADS))
        g = -jnp.exp(a_log) * jax.nn.softplus(pa.reshape(pa.shape[0], T, N_DIR, DN_HEADS) + dt_bias)
        return q_d, k_d, v_d, g, beta

    s_zero = jnp.zeros((B, DN_HEADS, DN_HEAD_DIM, DN_HEAD_DIM), jnp.float32)
    o_dc, s_cf, s_cb = bidir_delta(*dn_inputs(cdq, cdk, cdv, cda, cdb), s_zero, s_zero)
    o_dl, _, _ = bidir_delta(*dn_inputs(dq, dk, dv, da, db), s_cf, s_cb)

    def merge(y_a, o_d, z, gate_a, gate_d):
        y_d = (rms_norm_2(o_d, dn_norm_g) * jax.nn.silu(heads(z, DN_HEADS))).reshape(z.shape)
        y = jax.nn.sigmoid(gate_a) * (y_a @ w_br_attn) + jax.nn.sigmoid(gate_d) * (y_d @ w_br_dn)
        return y @ w_out

    def mlp(s, shift, scale_m):
        hm = rms_norm_2(s, g_norm2) * (1.0 + scale_m) + shift
        return jnp.square(jax.nn.relu(hm @ w_mlp1)) @ w_mlp2

    x_new = x.astype(jnp.float32) + gt1 * merge(y_attn, o_dl, dz, ga, gd)
    x_new = x_new + gt2 * mlp(x_new, sh2, sc2)

    if update_ctx:
        q_ac = rms_norm_2(heads(caq, ATTN_Q_HEADS), q_norm_g)
        y_attn_c = ctx_self_attention(q_ac, k_ac, v_ac, attn_sink)
        ctx = ctx.astype(jnp.float32) + cgt1 * merge(y_attn_c, o_dc, cdz, cga, cgd)
        ctx = ctx + cgt2 * mlp(ctx, csh2, csc2)
    return x_new, ctx

def second_inputs(seed: int = 0) -> dict:
    key = jax.random.key(seed)
    ks = jax.random.split(key, 24)
    f32 = jnp.float32
    nrm = lambda k, shape, s: jax.random.normal(k, shape, f32) * s
    dt = jnp.exp(jax.random.uniform(ks[12], (DEPTH, N_DIR, DN_HEADS), f32, np.log(1e-3), np.log(1e-1)))
    return {
        "x": nrm(ks[0], (BATCH, SEQ, D_MODEL), 1.0),
        "c": nrm(ks[1], (BATCH, D_MODEL), 1.0),
        "ctx": nrm(ks[2], (BATCH, CTX_LEN, D_MODEL), 1.0),
        "c_ctx": nrm(ks[3], (D_MODEL,), 1.0),
        "w_ada": nrm(ks[4], (DEPTH, D_MODEL, 6 * D_MODEL), 0.5 * D_MODEL ** -0.5),
        "b_ada": nrm(ks[5], (DEPTH, 6 * D_MODEL), 0.02),
        "g_norm1": 1.0 + nrm(ks[6], (DEPTH, D_MODEL), 0.1),
        "w_in": nrm(ks[7], (DEPTH, D_MODEL, IN_WIDTH), D_MODEL ** -0.5),
        "q_norm_g": 1.0 + nrm(ks[8], (DEPTH, HEAD_DIM), 0.1),
        "k_norm_g": 1.0 + nrm(ks[9], (DEPTH, HEAD_DIM), 0.1),
        "attn_sink": nrm(ks[10], (DEPTH, ATTN_Q_HEADS), 0.5),
        "conv_w": nrm(ks[11], (DEPTH, CONV_W_2, 3 * DN_WIDTH), CONV_W_2 ** -0.5),
        "a_log": jnp.log(jax.random.uniform(ks[13], (DEPTH, N_DIR, DN_HEADS), f32, 1.0, 16.0)),
        "dt_bias": dt + jnp.log(-jnp.expm1(-dt)),
        "dn_norm_g": 1.0 + nrm(ks[14], (DEPTH, DN_HEAD_DIM), 0.1),
        "w_br_attn": nrm(ks[15], (DEPTH, ATTN_WIDTH, D_MODEL), ATTN_WIDTH ** -0.5),
        "w_br_dn": nrm(ks[16], (DEPTH, DN_WIDTH, D_MODEL), DN_WIDTH ** -0.5),
        "w_out": nrm(ks[17], (DEPTH, D_MODEL, D_MODEL), D_MODEL ** -0.5),
        "g_norm2": 1.0 + nrm(ks[18], (DEPTH, D_MODEL), 0.1),
        "w_mlp1": nrm(ks[19], (DEPTH, D_MODEL, D_FF_2), D_MODEL ** -0.5),
        "w_mlp2": nrm(ks[20], (DEPTH, D_FF_2, D_MODEL), D_FF_2 ** -0.5),
    }

def second_block(x, c, ctx, c_ctx, w_ada, b_ada, g_norm1, w_in, q_norm_g, k_norm_g, attn_sink, conv_w,
              a_log, dt_bias, dn_norm_g, w_br_attn, w_br_dn, w_out, g_norm2, w_mlp1, w_mlp2):
    out_dtype = x.dtype
    for layer in range(DEPTH):
        x, ctx = trunk_layer(x, ctx, c, c_ctx, w_ada[layer], b_ada[layer], g_norm1[layer], w_in[layer],
                             q_norm_g[layer], k_norm_g[layer], attn_sink[layer], conv_w[layer],
                             a_log[layer], dt_bias[layer], dn_norm_g[layer], w_br_attn[layer],
                             w_br_dn[layer], w_out[layer], g_norm2[layer], w_mlp1[layer], w_mlp2[layer],
                             update_ctx=layer < DEPTH - 1)
    return x.astype(out_dtype)


def setup_inputs(seed=0):
    out = dict(first_inputs(seed))
    for name, value in second_inputs(seed + 1).items():
        if name != "x":
            out[name + "_2"] = value
    return out


def reference(
    x, ln1_g, w_in, b_in, rpb, w_att_o, conv_w, conv_b, w_rg_a, b_rg_a, w_rg_i, b_rg_i,
    lru_lambda, w_rec_o, w_out, ln2_g, w_ff1, w_ff2, lnf_g, c_2, ctx_2, c_ctx_2, w_ada_2,
    b_ada_2, g_norm1_2, w_in_2, q_norm_g_2, k_norm_g_2, attn_sink_2, conv_w_2, a_log_2,
    dt_bias_2, dn_norm_g_2, w_br_attn_2, w_br_dn_2, w_out_2, g_norm2_2, w_mlp1_2, w_mlp2_2,
):
    x = first_block(
        x, ln1_g, w_in, b_in, rpb, w_att_o, conv_w, conv_b, w_rg_a, b_rg_a, w_rg_i, b_rg_i,
        lru_lambda, w_rec_o, w_out, ln2_g, w_ff1, w_ff2, lnf_g,
    )
    return second_block(
        x, c_2, ctx_2, c_ctx_2, w_ada_2, b_ada_2, g_norm1_2, w_in_2, q_norm_g_2, k_norm_g_2,
        attn_sink_2, conv_w_2, a_log_2, dt_bias_2, dn_norm_g_2, w_br_attn_2, w_br_dn_2, w_out_2,
        g_norm2_2, w_mlp1_2, w_mlp2_2,
    )


_drawn_inputs = setup_inputs


def setup_inputs(seed=0):
    import zlib

    import numpy as np

    out = dict(_drawn_inputs(seed))
    spreads = {}
    factors = {'rpb': 8.0,
     'b_rg_a': 8.0,
     'b_rg_i': 8.0,
     'ctx_2': 5.079,
     'g_norm1_2': 2.905,
     'q_norm_g_2': 8.0,
     'k_norm_g_2': 8.0,
     'attn_sink_2': 8.0,
     'dn_norm_g_2': 5.192}
    for name, (base, spread) in spreads.items():
        noise = np.random.default_rng([zlib.crc32(name.encode()), seed]).standard_normal(out[name].shape)
        drawn = base * np.exp(spread * noise) if base else spread * noise
        out[name] = __import__('jax').numpy.asarray(drawn.astype(out[name].dtype))
    for name, factor in factors.items():
        out[name] = (out[name] * factor).astype(out[name].dtype)
    return out
```

```python
from contextlib import ExitStack

import numpy as np

import concourse.bass as bass
from concourse import mybir

F32 = mybir.dt.float32
ALU = mybir.AluOpType
ACT = mybir.ActivationFunctionType
AX = mybir.AxisListType
P = 128
S = 1024
CTX = 256
EPS = 1e-6
GC = 0.7978845608028654
VEC = {}
VN = [0]
for _n, _w in [("ln1", 8), ("ln2", 8), ("bq", 4), ("bk", 4), ("bu", 8), ("by", 8), ("bga", 8), ("bgr", 8),
               ("cw", 32), ("cb", 8), ("ba", 16), ("bi", 16), ("lam", 16), ("c2", 16), ("bada", 48),
               ("g1", 8), ("g2", 8), ("cw2", 36)]:
    VEC[_n] = (VN[0], _w)
    VN[0] += _w
NVEC = VN[0]
ROW = {}
RN = [0]
for _n, _w in [("bv", 512), ("lnf", 1024), ("qk", 640), ("dn", 512), ("dt", 16), ("al", 16), ("sink", 8)]:
    ROW[_n] = (RN[0], _w)
    RN[0] += _w
NROW = RN[0]
LEVELS = 7

def shape_constants():
    i = np.arange(128)
    c = {}
    c["ident"] = np.eye(128, dtype=np.float32)
    lv = np.zeros((128, 2, LEVELS, 128), np.float32)
    for k in range(LEVELS):
        m = 1 << k
        same = (i[:, None] // (2 * m)) == (i[None, :] // (2 * m))
        lo = (i // m) % 2 == 0
        hi = ~lo
        lv[:, 0, k, :] = same & lo[:, None] & hi[None, :]
        lv[:, 1, k, :] = same & hi[:, None] & lo[None, :]
    c["lv"] = lv.reshape(128, -1)
    cum = np.zeros((128, 2, 128), np.float32)
    cum[:, 0, :] = i[:, None] <= i[None, :]
    cum[:, 1, :] = i[:, None] >= i[None, :]
    c["cum"] = cum.reshape(128, -1)
    neg = np.where(cum > 0, 0.0, -1e30).astype(np.float32)
    c["neg"] = neg.reshape(128, -1)
    wn = np.zeros((128, 3, 128), np.float32)
    wn[:, 0, :] = np.where(i[None, :] >= i[:, None], 0.0, -1e30)
    wn[:, 2, :] = np.where(i[None, :] <= i[:, None], 0.0, -1e30)
    c["wn"] = wn.reshape(128, -1)
    pos = np.arange(S)
    fr = (np.float32(10000.0) ** (-np.arange(16, dtype=np.float32) / np.float32(16))).astype(np.float32)
    ar = (pos // 64).astype(np.float32)[:, None] * fr
    ac = (pos % 64).astype(np.float32)[:, None] * fr
    cos = np.concatenate([np.cos(ar), np.cos(ar), np.cos(ac), np.cos(ac)], 1)
    sin = np.concatenate([-np.sin(ar), np.sin(ar), -np.sin(ac), np.sin(ac)], 1)
    rope = np.concatenate([cos, sin], 1).astype(np.float32)
    c["rope"] = np.ascontiguousarray(rope.reshape(8, 128, 128).transpose(1, 0, 2)).reshape(128, -1)
    q = np.arange(64)
    ws = np.clip(q - 8, 0, 48)
    k = np.arange(64)
    nm = np.where((k[None, :] >= ws[:, None]) & (k[None, :] < ws[:, None] + 16), 0.0, -1e30).astype(np.float32)
    c["nm"] = np.concatenate([nm, nm], 0)
    return c

CONST = [("ident", 128), ("lv", 2 * LEVELS * 128), ("cum", 256), ("neg", 256), ("wn", 384), ("rope", 1024), ("nm", 64)]

class Said:

    def matmul(self, *a, **k):
        return lambda e: e.matmul(*a, **k)

    def transpose(self, *a, **k):
        return lambda e: e.transpose(*a, **k)

    def activation(self, *a, **k):
        return lambda e: e.activation(*a, **k)

    def tensor_tensor(self, *a, **k):
        return lambda e: e.tensor_tensor(*a, **k)

    def tensor_scalar(self, *a, **k):
        return lambda e: e.tensor_scalar(*a, **k)

    def scalar_tensor_tensor(self, *a, **k):
        return lambda e: e.scalar_tensor_tensor(*a, **k)

    def tensor_tensor_scan(self, *a, **k):
        return lambda e: e.tensor_tensor_scan(*a, **k)

    def tensor_copy(self, *a, **k):
        return lambda e: e.tensor_copy(*a, **k)

    def tensor_reduce(self, *a, **k):
        return lambda e: e.tensor_reduce(*a, **k)

    def reciprocal(self, *a, **k):
        return lambda e: e.reciprocal(*a, **k)

    def memset(self, *a, **k):
        return lambda e: e.memset(*a, **k)

SAID = Said()

class Queue:

    def __init__(self, nc, ctx, name):
        self.sem = ctx.enter_context(nc.semaphore("s_" + name))
        self.items, self.n, self.seen = [], 0, {}

    def wait(self, *toks):
        for t in toks:
            if t is None:
                continue
            if isinstance(t, list):
                self.wait(*t)
                continue
            sem, val = t
            if self.seen.get(id(sem), 0) < val:
                self.seen[id(sem)] = val
                self.items.append(lambda e, sem=sem, val=val: e.wait_ge(sem, val))

    def __call__(self, fn, *toks):
        self.wait(*toks)
        self.n += 1
        issue = fn(SAID)
        self.items.append(lambda e: issue(e).then_inc(self.sem, 1))
        return (self.sem, self.n)

    def quiet(self, fn, *toks):
        self.wait(*toks)
        self.items.append(fn(SAID))

    def dma(self, out, in_, stream, *toks):
        self.wait(*toks)
        stream[1] += 16
        sem, val = stream
        self.items.append(lambda e: e.dma_start(out, in_).then_inc(sem, 16))
        return (sem, val)

    def last(self):
        return (self.sem, self.n) if self.n else None

    def replay(self, e):
        for it in self.items:
            it(e)

class Pool_:

    def __init__(self, places):
        self.free = [(p, None) for p in places]

    def take(self):
        return self.free.pop(0)

    def give(self, place, *toks):
        self.free.append((place, list(toks)))

def pipeline(n, stages, lags=None):
    lags = lags or list(range(len(stages)))
    for i in range(n + max(lags)):
        for st, lag in zip(stages, lags):
            if 0 <= i - lag < n:
                st(i - lag)

def build(nc, d, out, dbg=None, upto=99):
    dbg = dbg or {}
    ctx = ExitStack()
    with ctx:
        def stream(name):
            return [ctx.enter_context(nc.semaphore(name)), 0]

        pe, dve, act, gp, sp = (Queue(nc, ctx, n) for n in ("pe", "dve", "act", "gp", "sp"))
        A = ctx.enter_context(nc.sbuf_tensor("arena", [P, 52480], F32))
        ident = ctx.enter_context(nc.sbuf_tensor("identm", [P, 128], F32))
        vec = ctx.enter_context(nc.sbuf_tensor("vec", [P, NVEC], F32))
        sm = ctx.enter_context(nc.sbuf_tensor("sm", [P, 64], F32))
        PS = [ctx.enter_context(nc.psum_tensor(f"ps{i}", [P, 512], F32)) for i in range(8)]
        banks = Pool_(range(8))
        W0, HT0, F0, CB = 0, 12288, 22528, 48640
        F1, F2 = F0 + 8192, F0 + 16384
        xs = nc.dram_tensor("x_stash", [S, 1024], F32, kind="Internal").ap()

        def R(off, n):
            return A[:, off:off + n]

        def R3(off, a, b):
            return A[:, off:off + a * b].rearrange("p (a b) -> p a b", a=a)

        def V(name, j, n=1):
            o = VEC[name][0] + j
            return vec[:, o:o + n]

        def everyone():
            return [q.last() for q in (pe, dve, act, gp)]

        def bc(ap, shape):
            return ap.to_broadcast(shape)

        ldvec = stream("ldvec")
        t_vec = sp.dma(vec[:, :], d["vecs"], ldvec)
        t_id = sp.dma(ident[:, :], d["ident"], stream("ldid"))
        misc = [stream(f"misc{i}") for i in range(24)]

        def load(dst, src, *toks, q=None):
            return (q or sp).dma(dst, src, misc.pop(0), *toks)

        def dump(name, ap, *toks):
            if name in dbg:
                dbg[name][1] = sp.dma(dbg[name][0], ap, stream("dbg" + name), *toks)
                for q in (pe, dve, act, gp):
                    q.wait(dbg[name][1])

        wring = Pool_(range(3))
        wsem = [stream(f"w{i}") for i in range(3)]

        def strip(src, kt, n, *toks):
            slot, free = wring.take()
            view = R3(W0 + slot * 4096, kt, n)
            tok = sp.dma(view, src.rearrange("(k p) n -> p k n", p=P), wsem[slot], free, *toks)
            return slot, view, tok

        HT = R3(HT0, 8, 1280)

        def accumulate(out_ap, pairs, toks, start=True, stop=True):
            n = len(pairs)
            for i, (l, r) in enumerate(pairs):
                def mm(e, l=l, r=r, i=i):
                    return e.matmul(out_ap, l, r, start=start and i == 0, stop=stop and i == n - 1)
                if i < n - 1:
                    pe.quiet(mm, *(toks if i == 0 else ()))
                else:
                    tok = pe(mm, *(toks if i == 0 else ()))
            return tok

        def dense_fm(st, rhs, pieces, evac, tok_r, kt=8, mts=None):
            slot, w, tw = st
            for m in (range(4) if mts is None else mts):
                for n0, N in pieces:
                    b, free = banks.take()
                    o = PS[b][:, 0:N]
                    tok = accumulate(o, [(w[:, k, m * 128:(m + 1) * 128], rhs(k, n0, N)) for k in range(kt)],
                                     (free, tw, tok_r))
                    banks.give(b, evac(m, n0, N, o, tok))
            return tok

        def dense_tm(st, lhs, tiles, N, evac, tok_r, c0=0, kt=8):
            slot, w, tw = st
            for t in tiles:
                b, free = banks.take()
                o = PS[b][:, 0:N]
                tok = accumulate(o, [(lhs(k, t), w[:, k, c0:c0 + N]) for k in range(kt)], (free, tw, tok_r))
                banks.give(b, evac(t, o, tok))
            return tok

        def done(st, tok):
            wring.give(st[0], tok)

        hrhs = lambda k, n0, N: HT[:, k, n0:n0 + N]
        hlhs = lambda k, t: HT[:, k, t * 128:(t + 1) * 128]
        HALVES = [(0, 512), (512, 512)]

        def norm_stats(X, nt, ss, junk, tok_x, width=1024):
            for t in range(nt):
                tk = act(lambda e, t=t: e.activation(junk, X(t), ACT.Square, accum_out=ss[:, t:t + 1]),
                         tok_x, act.last())
            tk = dve(lambda e: e.tensor_scalar(ss, ss, 1.0 / width, EPS, ALU.mult, ALU.add), tk)
            tk = act(lambda e: e.activation(ss, ss, ACT.Sqrt), tk)
            return dve(lambda e: e.reciprocal(ss, ss), tk)

        def norm_T(X, nt, ss, xn, gcol, scol, h0, tok, tok_ht):
            toks = []
            for h in range(0, nt, 4):
                n4 = min(4, nt - h)
                place, free = xn.take()
                for t in range(n4):
                    tn = dve(lambda e, t=t, h=h, place=place: e.tensor_scalar(
                        place[:, t, :], X(h + t), ss[:, h + t:h + t + 1], None, ALU.mult), tok, free)
                for k in range(8):
                    b, fb = banks.take()
                    for t in range(n4):
                        tp = pe(lambda e, b=b, t=t, k=k, place=place: e.transpose(
                            PS[b][:, t * 128:(t + 1) * 128], place[:, t, k * 128:(k + 1) * 128], ident[:, :]),
                            fb, tn, t_id)
                    dst = HT[:, k, h0 + h * 128:h0 + (h + n4) * 128]
                    if k % 2:
                        te = dve(lambda e, b=b, k=k, dst=dst, n4=n4: e.tensor_scalar(
                            dst, PS[b][:, 0:n4 * 128], gcol(k), scol(k) if scol else None, ALU.mult,
                            ALU.add if scol else ALU.bypass), tp, tok_ht)
                    else:
                        te = act(lambda e, b=b, k=k, dst=dst, n4=n4: e.activation(
                            dst, PS[b][:, 0:n4 * 128], ACT.Identity, scale=gcol(k),
                            bias=scol(k) if scol else 0.0), tp, tok_ht)
                    banks.give(b, te)
                    toks.append(te)
                xn.give(place, tp)
            return toks[-2:]

        X = R3(F0, 8, 1024)
        Xt = lambda t: X[:, t, :]
        t_x = sp.dma(X, d["x"].rearrange("(t p) n -> p t n", p=P), stream("ldx"))
        xn = Pool_([R3(F1, 4, 1024), R3(F1 + 4096, 4, 1024)])
        rs = sm[:, 0:8]
        tk = norm_stats(Xt, 8, rs, R(F2, 1024), t_x)
        t_h = norm_T(Xt, 8, rs, xn, lambda k: V("ln1", k), None, 0, [tk, t_vec], None)
        dump("h1", HT[:, :, 0:1024], t_h)

        w_in = d["w_in"]
        QB = A[:, F0:F0 + 8192].rearrange("p (j r s q) -> p j r s q", j=4, r=16, s=2)
        KT = R3(F1, 4, 1024)
        VT = R3(F1 + 4096, 8, 512)
        VS = R3(F2, 7, 512)
        BI = R3(CB, 4, 960)
        phase = everyone()
        tz = gp(lambda e: e.memset(R(F0, 8192), 0.0), phase)
        nm = R(F2 + 3584, 64)
        bvr = R(F2 + 3648, 512)
        t_nm = load(nm, d["nm"], phase)
        t_bv = load(bvr, d["rows"][:, ROW["bv"][0]:ROW["bv"][0] + 512], phase)
        t_bi = load(BI, d["nbias"], phase)
        for j in range(4):
            t_bi2 = gp(lambda e, j=j: e.tensor_tensor(
                BI[:, j, :].rearrange("p (a k) -> p a k", k=64), BI[:, j, :].rearrange("p (a k) -> p a k", k=64),
                bc(nm.unsqueeze(1), [P, 15, 64]), ALU.add), t_bi, t_nm)

        def ev_q(m, n0, N, o, tok):
            for s in range(2):
                rows = slice(64 * s, 64 * s + 64)
                tk = dve(lambda e, s=s, rows=rows: e.tensor_scalar(
                    QB[rows, m, n0 // 64:(n0 + N) // 64, s, :], o[rows].rearrange("p (r q) -> p r q", q=64),
                    V("bq", m)[rows], 0.125, ALU.add, ALU.mult), tok, tz)
            return tk

        def ev_k(m, n0, N, o, tok):
            return act(lambda e: e.activation(KT[:, m, n0:n0 + N], o, ACT.Identity, bias=V("bk", m)), tok, phase)

        st = strip(w_in[:, 0:512], 8, 512)
        done(st, dense_fm(st, hrhs, HALVES, ev_q, t_h))
        st = strip(w_in[:, 512:1024], 8, 512)
        done(st, dense_fm(st, hrhs, HALVES, ev_k, t_h))
        st = strip(w_in[:, 1024:1536], 8, 512)
        done(st, dense_tm(st, hlhs, range(8), 512,
                          lambda t, o, tok: dve(lambda e: e.tensor_tensor(VT[:, t, :], o, bvr, ALU.add), tok, t_bv, phase),
                          t_h))
        vsst = stream("vshift")
        tv = dve.last()
        act.dma(VS[0:64, :, :], VT[64:128, 0:7, :], vsst, tv, phase)
        t_vs = act.dma(VS[64:128, :, :], VT[0:64, 1:8, :], vsst)

        T0 = F2 + 4160
        sb = Pool_([R(T0 + i * 512, 512) for i in range(3)])
        pbuf = Pool_([R(T0 + 1536 + i * 512, 512) for i in range(3)])
        ptb = Pool_([R3(T0 + 3072 + i * 512, 4, 128) for i in range(3)])
        st1 = {}
        tqk = [dve.last(), act.last()]
        statn = sm[:, 8:32].rearrange("p (a b) -> p a b", b=3)

        def natt_scores(i):
            r, j = divmod(i, 4)
            start = min(max(r - 4, 0), 8)
            b, free = banks.take()
            tok = accumulate(PS[b][:, :], [(QB[:, j, r, :, :], KT[:, j, start * 64:start * 64 + 512])], (free, tqk))
            off = start - r + 7
            sbt, fs = sb.take()
            tk = dve(lambda e: e.tensor_tensor(sbt, PS[b][:, :], BI[:, j, off * 64:off * 64 + 512], ALU.add),
                     tok, fs, t_bi2)
            banks.give(b, tk)
            c = statn[:, i % 8, :]
            tk = dve(lambda e: e.tensor_reduce(c[:, 0:1], sbt, AX.X, ALU.max, negate=True), tk)
            pt, fp = pbuf.take()
            te = act(lambda e: e.activation(pt, sbt, ACT.Exp, bias=c[:, 0:1], accum_out=c[:, 1:2]), tk, fp)
            sb.give(sbt, te)
            tk = dve(lambda e: e.reciprocal(c[:, 2:3], c[:, 1:2]), te)
            st1[i] = (pt, c, tk, start)

        def natt_scale(i):
            pt, c, tk, start = st1[i]
            tk = gp(lambda e: e.tensor_scalar(pt, pt, c[:, 2:3], None, ALU.mult), tk)
            st1[i] = (pt, tk, start)

        def natt_tr(i):
            pt, tk, start = st1[i]
            b, free = banks.take()
            for c in range(4):
                tp = pe(lambda e, c=c: e.transpose(PS[b][:, c * 128:(c + 1) * 128], pt[:, c * 128:(c + 1) * 128],
                                                   ident[:, :]), tk, free)
            pbuf.give(pt, tp)
            q, fq = ptb.take()
            te = act(lambda e: e.activation(q, PS[b][:, :].rearrange("p (a b) -> p a b", a=4), ACT.Copy), tp, fq)
            banks.give(b, te)
            st1[i] = (q, te, start)

        def natt_pv(i):
            q, te, start = st1.pop(i)
            r, j = divmod(i, 4)
            b, free = banks.take()
            if start % 2:
                vv = [VS[:, start // 2 + c, j * 128:(j + 1) * 128] for c in range(4)]
            else:
                vv = [VT[:, start // 2 + c, j * 128:(j + 1) * 128] for c in range(4)]
            tok = accumulate(PS[b][:, 0:128], [(vv[c], q[:, c, :]) for c in range(4)], (te, free, t_vs))
            ptb.give(q, tok)
            t1 = dve(lambda e: e.tensor_copy(QB[0:64, j, r, 0, :], PS[b][0:64, 0:64]), tok)
            t2 = dve(lambda e: e.tensor_copy(QB[64:128, j, r, 0, :], PS[b][64:128, 64:128]), tok)
            banks.give(b, t2)

        pipeline(64, [natt_scores, natt_scale, natt_tr, natt_pv], [0, 0, 1, 2])
        YA = QB[:, :, :, 0, :]
        dump("yatt", YA, dve.last())
        t_ya = dve.last()

        RC = R3(F1, 8, 1024)
        phase = everyone()
        wrg = stream("wrg")
        hb = ctx.enter_context(nc.sbuf_tensor("hb", [P, 80], F32))
        th = dve(lambda e: e.tensor_scalar(hb[:, 0:32], V("ba", 0, 32), 0.5, None, ALU.mult), phase, t_vec)
        assert VEC["bi"][0] == VEC["ba"][0] + 16
        tk = act(lambda e: e.activation(hb[:, 32:48], V("lam", 0, 16), ACT.Abs), phase, t_vec)
        tk = act(lambda e: e.activation(hb[:, 32:48], hb[:, 32:48], ACT.Exp, scale=-1.0), tk)
        tk = act(lambda e: e.activation(hb[:, 32:48], hb[:, 32:48], ACT.Ln, bias=1.0), tk)
        t2 = dve(lambda e: e.tensor_scalar(hb[:, 48:64], V("lam", 0, 16), -1.0, 0.0, ALU.mult, ALU.max), th)
        t2 = dve(lambda e: e.tensor_tensor(hb[:, 32:48], hb[:, 32:48], hb[:, 48:64], ALU.add), tk, t2)
        t3 = dve(lambda e: e.tensor_scalar(hb[:, 32:48], hb[:, 32:48], 4.0, None, ALU.mult), t2)
        t3 = dve(lambda e: e.tensor_scalar(hb[:, 48:64], hb[:, 32:48], -1.0, None, ALU.mult), t3)
        tk = dve(lambda e: e.tensor_scalar(hb[:, 64:80], V("bga", 0, 16), 0.5, None, ALU.mult), t_vec)
        assert VEC["bgr"][0] == VEC["bga"][0] + 8
        t_hb = dve.last()

        B0 = F2
        ub = [R(B0 + i * 1032, 1028) for i in range(2)]
        rb = B0 + 2064
        uc_, y_, t1_, a_, s_, iu_, hf_ = (R(rb + i * 1024, 1024) for i in range(7))
        hb_ = R(CB, 1024)
        t2_ = R(CB + 1024, 1024)
        gw = [R3(CB + 2048 + i * 512, 4, 128) for i in range(2)]
        gwd = stream("gw0"), stream("gw1")
        tz = None
        for i in range(2):
            tz = gp(lambda e, i=i: e.memset(ub[i][:, 0:2], 0.0), phase)
            tz = gp(lambda e, i=i: e.memset(ub[i][:, 1026:1028], 0.0), phase)
            tz = gp(lambda e, i=i: e.memset(gw[i], 0.0), phase)
        urel = [None, None]
        gwrel = [None, None]
        rsc = {}
        strips = {}

        def rec_in(t):
            c = t // 4
            if t % 4 == 0:
                strips["u"] = strip(w_in[:, 1536 + c * 512:2048 + c * 512], 8, 512)
                strips["y"] = strip(w_in[:, 2560 + c * 512:3072 + c * 512], 8, 512)
            u = ub[t % 2]
            g = gw[t % 2]
            for s in range(2):
                for w, nm_ in enumerate(("w_rg_a", "w_rg_i")):
                    for dd in range(2):
                        tg = act.dma(g[64 * s:64 * s + 64, dd * 2 + w, 64 * s:64 * s + 64],
                                     d[nm_][dd, 2 * t + s, :, :], gwd[t % 2], tz, gwrel[t % 2])
            tok = dense_fm(strips["u"], hrhs, HALVES,
                     lambda m, n0, N, o, tk: act(lambda e: e.activation(
                         u[:, 2 + n0:2 + n0 + N], o, ACT.Identity, bias=V("bu", t)), tk, tz, urel[t % 2], t_hb),
                     t_h, mts=[t % 4])
            tu = act.last()
            tok = dense_fm(strips["y"], hrhs, HALVES,
                           lambda m, n0, N, o, tk: act(lambda e: e.activation(
                               y_[:, n0:n0 + N], o, ACT.Identity, bias=V("by", t)), tk, rsc.get("y")),
                           t_h, mts=[t % 4])
            ty = act.last()
            if t % 4 == 3:
                done(strips["u"], tok)
                done(strips["y"], tok)
            rsc[t] = (tg, tu, ty)

        def rec_tile(t):
            tg, tu, ty = rsc.pop(t)
            u = ub[t % 2]
            g = gw[t % 2]
            cw = lambda j: V("cw", j * 8 + t)
            k1 = dve(lambda e: e.tensor_tensor(t1_, y_, y_, ALU.mult), ty, rsc.get("t1"))
            k1 = dve(lambda e: e.tensor_scalar(t1_, t1_, 0.044715, 1.0, ALU.mult, ALU.add), k1)
            k1 = dve(lambda e: e.tensor_tensor(t1_, t1_, y_, ALU.mult), k1)
            k2 = act(lambda e: e.activation(t1_, t1_, ACT.Tanh, scale=GC), k1)
            k = dve(lambda e: e.tensor_scalar(uc_, u[:, 0:1024], cw(0), V("cb", t), ALU.mult, ALU.add), tu,
                    rsc.get("uc"))
            for j in range(1, 4):
                k = dve(lambda e, j=j: e.scalar_tensor_tensor(out=uc_, in0=u[:, j:j + 1024], scalar=cw(j), in1=uc_,
                                                              op0=ALU.mult, op1=ALU.add), k)
            urel[t % 2] = k
            tuc = k
            k1 = dve(lambda e: e.scalar_tensor_tensor(out=t1_, in0=t1_, scalar=1.0, in1=y_, op0=ALU.add,
                                                      op1=ALU.mult), k2)
            rsc["y"] = k1
            for dd in range(2):
                h = hf_ if dd == 0 else hb_
                for w, (dst, bo) in enumerate(((a_, dd * 8 + t), (iu_, 16 + dd * 8 + t))):
                    for n0, N in HALVES:
                        b, free = banks.take()
                        tok = accumulate(PS[b][:, :], [(g[:, dd * 2 + w, :], uc_[:, n0:n0 + N])], (free, tg, tuc))
                        k = act(lambda e, b=b, dst=dst, bo=bo, n0=n0: e.activation(
                            dst[:, n0:n0 + 512], PS[b][:, :], ACT.Tanh, scale=0.5, bias=hb[:, bo:bo + 1]), tok,
                            rsc.get("a" if w == 0 else "iu"))
                        banks.give(b, k)
                    if w == 0:
                        ka = k
                kp, kn = hb[:, 32 + dd * 8 + t:33 + dd * 8 + t], hb[:, 48 + dd * 8 + t:49 + dd * 8 + t]
                ks = act(lambda e, kp=kp: e.activation(s_, a_, ACT.Tanh, scale=kp, bias=kp), ka, rsc.get("s"))
                ke = act(lambda e, kn=kn: e.activation(a_, a_, ACT.Exp, scale=kn, bias=kn), ks)
                kq = dve(lambda e: e.tensor_tensor(t2_, a_, a_, ALU.mult), ke, rsc.get("t2"))
                kq = dve(lambda e: e.scalar_tensor_tensor(out=s_, in0=t2_, scalar=1.0, in1=s_, op0=ALU.add,
                                                          op1=ALU.mult), kq)
                ks = act(lambda e: e.activation(s_, s_, ACT.Sqrt, scale=0.25), kq)
                ki = dve(lambda e: e.scalar_tensor_tensor(out=iu_, in0=iu_, scalar=1.0, in1=uc_, op0=ALU.add,
                                                          op1=ALU.mult), k)
                ki = dve(lambda e: e.tensor_tensor(iu_, iu_, s_, ALU.mult), ki, ks)
                rsc["s"] = ki
                if dd == 0:
                    kh = dve(lambda e, h=h: e.tensor_tensor_scan(h, a_, iu_, 0.0, ALU.mult, ALU.add), ki, rsc.get("h"))
                else:
                    kh = dve(lambda e, h=h: e.tensor_tensor_scan(h[:, ::-1], a_[:, ::-1], iu_[:, ::-1], 0.0, ALU.mult,
                                                                 ALU.add), ki, rsc.get("h"))
                rsc["a"] = rsc["iu"] = kh
            rsc["t2"] = kq
            rsc["uc"] = kh
            gwrel[t % 2] = tok
            k = dve(lambda e: e.tensor_tensor(hf_, hf_, hb_, ALU.add), kh)
            k = dve(lambda e: e.scalar_tensor_tensor(out=RC[:, t, :], in0=hf_, scalar=0.5, in1=t1_, op0=ALU.mult,
                                                     op1=ALU.mult), k, phase)
            rsc["h"] = rsc["t1"] = k

        pipeline(8, [rec_in, rec_tile], [0, 0])
        t_rc = dve.last()
        dump("rec", RC, t_rc)

        def sigmoid_mix(MX, src_att, kt_att, rhs_att, src_gate, bcol, first, tok_r, tmp, tok_prev, att=None):
            for c in range(2):
                sa = att or strip(src_att(c), kt_att, 512)
                sg = strip(src_gate(c), 8, 512)
                for m in range(4):
                    for n0, N in HALVES:
                        mo = c * 4 + m
                        b, free = banks.take()
                        tok = accumulate(PS[b][:, :], [(sg[1][:, k, m * 128:(m + 1) * 128], hrhs(k, n0, N))
                                                       for k in range(8)], (free, sg[2], t_hx[0]))
                        tt, ft = tmp.take()
                        ka = act(lambda e, b=b, tt=tt, mo=mo: e.activation(
                            tt, PS[b][:, :], ACT.Tanh, scale=0.5, bias=bcol(mo) if bcol else 0.0), tok, ft, tok_prev)
                        banks.give(b, ka)
                        b, free = banks.take()
                        mc = (c * 4 + m if att else m)
                        tok = accumulate(PS[b][:, :], [(sa[1][:, k, mc * 128:mc * 128 + 128], rhs_att(k, n0, N))
                                                       for k in range(kt_att)], (free, sa[2], tok_r))
                        dst = MX[:, mo, n0:n0 + 512]
                        if first:
                            k = dve(lambda e, b=b, tt=tt, dst=dst: e.scalar_tensor_tensor(
                                out=dst, in0=tt, scalar=1.0, in1=PS[b][:, :], op0=ALU.add, op1=ALU.mult), tok, ka,
                                tok_prev)
                            banks.give(b, k)
                        else:
                            k = dve(lambda e, b=b, tt=tt: e.scalar_tensor_tensor(
                                out=tt, in0=tt, scalar=1.0, in1=PS[b][:, :], op0=ALU.add, op1=ALU.mult), tok, ka)
                            banks.give(b, k)
                            k = gp(lambda e, tt=tt, dst=dst: e.tensor_tensor(dst, dst, tt, ALU.add), k)
                        tmp.give(tt, k)
                if not att:
                    done(sa, tok)
                done(sg, tok)
            return k

        t_hx = [t_h]
        MX = R3(F2, 8, 1024)
        phase = everyone()
        tmpx = Pool_([R(CB + i * 512, 512) for i in range(4)])
        wa = strip(d["w_att_o"], 4, 1024)
        sigmoid_mix(MX, None, 4, lambda k, n0, N: YA[:, k, n0 // 64:(n0 + N) // 64, :],
                    lambda c: w_in[:, 3584 + c * 512:4096 + c * 512], lambda m: hb[:, 64 + m:65 + m], True, t_ya, tmpx,
                    phase, att=wa)
        t_free0 = pe.last()
        done(wa, t_free0)
        k = sigmoid_mix(MX, lambda c: d["w_rec_o"][:, c * 512:(c + 1) * 512], 8,
                        lambda k, n0, N: RC[:, k, n0:n0 + N],
                        lambda c: w_in[:, 4608 + c * 512:5120 + c * 512], lambda m: hb[:, 72 + m:73 + m], False,
                        t_rc, tmpx, phase)
        dump("mix1", MX, k, dve.last())
        t_mx = [k, dve.last()]
        t_x = sp.dma(X, d["x"].rearrange("(t p) n -> p t n", p=P), stream("ldx2"), t_free0)

        def w_out_pass(src, X, MXv, t_mx, t_x, gate=None, tmp=None):
            for c in range(2):
                st = strip(src[:, c * 512:(c + 1) * 512], 8, 512)

                def ev(t, o, tok, c=c):
                    dst = X[:, t, c * 512:(c + 1) * 512]
                    if gate is None:
                        return dve(lambda e: e.scalar_tensor_tensor(out=dst, in0=o, scalar=0.5, in1=dst, op0=ALU.mult,
                                                                    op1=ALU.add), tok, t_x)
                    tt, ft = tmp.take()
                    k = dve(lambda e: e.scalar_tensor_tensor(out=tt, in0=o, scalar=0.5, in1=gate[0][:, c * 512:c * 512 + 512],
                                                             op0=ALU.mult, op1=ALU.mult), tok, ft, gate[1])
                    k2 = gp(lambda e: e.tensor_tensor(dst, dst, tt, ALU.add), k, t_x)
                    tmp.give(tt, k2)
                    return k
                done(st, dense_tm(st, lambda k, t: MXv[:, k, t * 128:(t + 1) * 128], range(8), 512, ev, t_mx))

        w_out_pass(d["w_out"], X, MX, t_mx, t_x)
        t_x = dve.last()
        dump("x1", X, t_x)

        mods = ctx.enter_context(nc.sbuf_tensor("mods", [P, 64], F32))
        sc2 = ctx.enter_context(nc.sbuf_tensor("sc2", [P, 16], F32))
        k = act(lambda e: e.activation(sc2[:, :], V("c2", 0, 16), ACT.Tanh, scale=0.5), t_vec)
        k = dve(lambda e: e.scalar_tensor_tensor(out=sc2[:, :], in0=sc2[:, :], scalar=1.0, in1=V("c2", 0, 16),
                                                 op0=ALU.add, op1=ALU.mult), k)
        t_sc = dve(lambda e: e.tensor_scalar(sc2[:, :], sc2[:, :], 0.5, None, ALU.mult), k)
        sc3 = sc2[:, :].rearrange("p (k b) -> p k b", b=2)

        def ada(s):
            st = strip(d["w_ada"][:, s * 512:(s + 1) * 512], 8, 512)
            nb = 2 if s < 4 else 1
            b, free = banks.take()
            for m in range(4):
                tok = accumulate(PS[b][:, m * 2:m * 2 + nb], [(st[1][:, k, m * 128:(m + 1) * 128], sc3[:, k, 0:nb])
                                                              for k in range(8)], (free, st[2], t_sc))
            done(st, tok)
            pv = PS[b][:, 0:8].rearrange("p (m b) -> p m b", b=2)
            k = dve(lambda e: e.tensor_tensor(mods[:, s * 4:s * 4 + 4], pv[:, :, 0], V("bada", s * 4, 4), ALU.add),
                    tok, t_vec)
            if nb == 2:
                k = dve(lambda e: e.tensor_tensor(mods[:, 48 + s * 4:52 + s * 4], pv[:, :, 1], V("bada", s * 4, 4),
                                                  ALU.add), tok)
            banks.give(b, k)

        def feed_forward(X, w1, w2, t_h, t_x, fb, tmp=None, gate=None, between=None):
            rel = [None, None]
            for q in range(4):
                f = fb[q % 2]
                for c in range(2):
                    st = strip(w1[:, q * 1024 + c * 512:q * 1024 + (c + 1) * 512], 8, 512)

                    def ev(m, n0, N, o, tok, c=c):
                        dst = f[:, c * 4 + m, n0:n0 + N]
                        k = act(lambda e: e.activation(dst, o, ACT.Relu), tok, rel[q % 2], phase)
                        gp(lambda e: e.tensor_tensor(dst, dst, dst, ALU.mult), k)
                        return k
                    done(st, dense_fm(st, hrhs, HALVES, ev, t_h))
                    if between:
                        between(q * 4 + c)
                tf = gp.last()
                for c in range(2):
                    st = strip(w2[q * 1024:(q + 1) * 1024, c * 512:(c + 1) * 512], 8, 512)

                    def ev2(t, o, tok, c=c):
                        dst = X[:, t, c * 512:(c + 1) * 512]
                        if gate is None:
                            return dve(lambda e: e.tensor_tensor(dst, dst, o, ALU.add), tok, t_x, dve.last())
                        tt, ft = tmp.take()
                        k = dve(lambda e: e.tensor_tensor(tt, o, gate[0][:, c * 512:c * 512 + 512], ALU.mult), tok, ft,
                                gate[1])
                        k = dve(lambda e: e.tensor_tensor(dst, dst, tt, ALU.add), k, t_x)
                        tmp.give(tt, k)
                        return k
                    tok = dense_tm(st, lambda k, t: f[:, k, t * 128:(t + 1) * 128], range(8), 512, ev2, tf)
                    done(st, tok)
                    if between:
                        between(q * 4 + 2 + c)
                rel[q % 2] = tok

        phase = everyone()
        xn = Pool_([R3(F1, 4, 1024), R3(F1 + 4096, 4, 1024)])
        tk = norm_stats(Xt, 8, rs, R(CB, 1024), [t_x, phase])
        t_h = norm_T(Xt, 8, rs, xn, lambda k: V("ln2", k), None, 0, [tk, phase], phase)
        t_hx[0] = t_h
        phase = everyone()
        FB = [R3(F1, 8, 1024), R3(F2, 8, 1024)]
        feed_forward(X, d["w_ff1"], d["w_ff2"], t_h, t_x, FB, between=lambda i: ada(i) if i < 12 else None)
        t_x = dve.last()
        phase = everyone()
        t_l = load(R(F2, 1024), d["rows"][:, ROW["lnf"][0]:ROW["lnf"][0] + 1024], phase)
        tk = norm_stats(Xt, 8, rs, R(CB, 1024), [t_x, phase])
        for t in range(8):
            t_x = dve(lambda e, t=t: e.scalar_tensor_tensor(out=X[:, t, :], in0=X[:, t, :], scalar=rs[:, t:t + 1],
                                                            in1=R(F2, 1024), op0=ALU.mult, op1=ALU.mult), tk, t_l)
        dump("xf", X, t_x)
        if upto < 2:
            return finish(nc, ctx, (pe, dve, act, gp, sp), out, X, t_x, dbg)

        phase = everyone()
        t_stash = sp.dma(xs.rearrange("(t p) n -> p t n", p=P), X, stream("stash"), t_x)
        gs = ctx.enter_context(nc.sbuf_tensor("gs", [P, 24], F32))
        t_gs = dve(lambda e: e.scalar_tensor_tensor(out=gs[:, 0:8], in0=mods[:, 8:16], scalar=1.0, in1=V("g1", 0, 8),
                                                    op0=ALU.add, op1=ALU.mult), dve.last())
        t_gs = dve(lambda e: e.scalar_tensor_tensor(out=gs[:, 8:16], in0=mods[:, 56:64], scalar=1.0, in1=V("g1", 0, 8),
                                                    op0=ALU.add, op1=ALU.mult))
        t_gs = dve(lambda e: e.scalar_tensor_tensor(out=gs[:, 16:24], in0=mods[:, 32:40], scalar=1.0,
                                                    in1=V("g2", 0, 8), op0=ALU.add, op1=ALU.mult))
        Cx = R3(F2, 2, 1024)
        t_c = load(Cx, d["ctx_2"].rearrange("(t p) n -> p t n", p=P), phase, t_x)
        xn = Pool_([R3(F1, 4, 1024), R3(F1 + 4096, 4, 1024)])
        rc = sm[:, 32:34]
        tk = norm_stats(Xt, 8, rs, R(CB, 1024), [t_x, phase])
        tk2 = norm_stats(lambda t: Cx[:, t, :], 2, rc, R(CB, 1024), [t_c, phase])
        ta = norm_T(Xt, 8, rs, xn, lambda k: gs[:, k:k + 1], lambda k: mods[:, k:k + 1], 0, [tk, phase, t_gs], [phase, t_gs])
        tb = norm_T(lambda t: Cx[:, t, :], 2, rc, xn, lambda k: gs[:, 8 + k:9 + k],
                    lambda k: mods[:, 48 + k:49 + k], 1024, [tk2, phase, t_gs], phase)
        t_h = [ta, tb]
        t_hx[0] = t_h
        dump("h2", HT[:, :, :], t_h)
        w2 = d["w_in_2"]

        phase = [everyone(), t_stash]
        kT = R3(F0, 4, 1280)
        qT = R3(F0 + 5120, 4, 1024)
        kt = R3(F0 + 9216, 10, 512)
        vt = R3(F0 + 14336, 10, 512)
        O = R3(F0 + 19456, 8, 512)
        XT = F0 + 23552
        lv = A[:, CB:CB + 1792].rearrange("p (d l f) -> p d l f", d=2, l=LEVELS)
        cum = R3(CB + 1792, 2, 128)
        neg = R3(CB + 2048, 2, 128)
        ones = R(CB + 2304, 128)
        AB = R3(CB + 2432, 10, 32)
        stb = R3(CB + 2752, 2, 32)
        rw = R(CB + 2816, 32)
        gneg = R3(CB + 2848, 10, 16)
        t_lv = load(lv, d["lv"], phase)
        t_cum = load(cum, d["cum"], phase)
        t_neg = load(neg, d["neg"], phase)
        t_rw = load(rw, d["rows"][:, ROW["dt"][0]:ROW["dt"][0] + 32], phase)
        t_one = gp(lambda e: e.memset(ones, 1.0), phase)
        st = strip(w2[:, 2816:2848], 8, 32)
        done(st, dense_tm(st, hlhs, range(10), 32,
                          lambda t, o, tok: act(lambda e: e.activation(AB[:, t, :], o, ACT.Copy), tok, phase), t_h))
        k = act.last()
        ka = act(lambda e: e.activation(rw[:, 16:32], rw[:, 16:32], ACT.Exp), t_rw)
        ga3 = AB[:, :, 0:16]
        be3 = AB[:, :, 16:32]
        tg1 = R3(XT, 10, 16)
        tg2 = R3(XT + 160, 10, 16)
        k1 = dve(lambda e: e.tensor_tensor(ga3, ga3, bc(rw[:, 0:16].unsqueeze(1), [P, 10, 16]), ALU.add), k, t_rw)
        k2 = act(lambda e: e.activation(tg1, ga3, ACT.Abs), k1)
        k2 = act(lambda e: e.activation(tg1, tg1, ACT.Exp, scale=-1.0), k2)
        k2 = act(lambda e: e.activation(tg1, tg1, ACT.Ln, bias=1.0), k2)
        k3 = dve(lambda e: e.tensor_scalar(tg2, ga3, 0.0, None, ALU.max), k1)
        k3 = dve(lambda e: e.tensor_tensor(tg2, tg2, tg1, ALU.add), k2, k3)
        k3 = dve(lambda e: e.tensor_tensor(gneg, tg2, bc(rw[:, 16:32].unsqueeze(1), [P, 10, 16]), ALU.mult), k3, ka)
        k3 = dve(lambda e: e.tensor_scalar(ga3, gneg, -1.0, None, ALU.mult), k3)
        k4 = act(lambda e: e.activation(be3, be3, ACT.Tanh, scale=0.5), k2)
        t_ab = dve(lambda e: e.tensor_scalar(be3, be3, 0.5, 0.5, ALU.mult, ALU.add), k4, k3)
        dump("ab", AB, t_ab)

        PIECES = [(0, 512), (512, 512), (1024, 256)]
        t0 = F0 + 19456
        raw = R(t0, 1288)
        xc = R(t0 + 1288, 1280)
        th_ = R(t0 + 2568, 1280)
        sq = R3(t0 + 3848, 10, 128)
        qt = R3(t0 + 5128, 10, 128)
        nr = R(CB + 3664, 20)
        tz = gp(lambda e: e.memset(raw, 0.0), phase)
        crel = {}
        for which, col in ((1, 1280), (0, 768), (2, 1792)):
            st = strip(w2[:, col:col + 512], 8, 512)
            pieces = PIECES if which else HALVES
            NT = 10 if which else 8
            segs = ((1, 0, 1024), (1027, 1024, 256)) if which else ((1, 0, 1024),)
            n_all = 1280 if which else 1024
            for m in range(4):
                def ev(mm, n0, N, o, tok):
                    off = 1 + n0 if n0 < 1024 else 1027 + n0 - 1024
                    return act(lambda e: e.activation(raw[:, off:off + N], o, ACT.Copy), tok, tz, crel.get("raw"))
                tok = dense_fm(st, hrhs, pieces, ev, t_h, mts=[m])
                tr = act.last()
                cwi = lambda j: V("cw2", j * 12 + which * 4 + m)
                for so, do, n in segs:
                    k = dve(lambda e, so=so, do=do, n=n, w=cwi(0): e.tensor_scalar(
                        xc[:, do:do + n], raw[:, so - 1:so - 1 + n], w, None, ALU.mult), tr, crel.get("xc"))
                    for j in (1, 2):
                        k = dve(lambda e, so=so, do=do, n=n, j=j, w=cwi(j): e.scalar_tensor_tensor(
                            out=xc[:, do:do + n], in0=raw[:, so - 1 + j:so - 1 + j + n], scalar=w,
                            in1=xc[:, do:do + n], op0=ALU.mult, op1=ALU.add), k)
                crel["raw"] = k
                k2 = act(lambda e, n=n_all: e.activation(th_[:, 0:n], xc[:, 0:n], ACT.Tanh, scale=0.5), k)
                k = dve(lambda e, n=n_all: e.scalar_tensor_tensor(out=xc[:, 0:n], in0=th_[:, 0:n], scalar=1.0,
                                                                  in1=xc[:, 0:n], op0=ALU.add, op1=ALU.mult), k2)
                got = []
                for h in range(0, NT, 4):
                    n4 = min(4, NT - h)
                    b, free = banks.take()
                    for t in range(n4):
                        tp = pe(lambda e, b=b, t=t, h=h: e.transpose(
                            PS[b][:, t * 128:(t + 1) * 128], xc[:, (h + t) * 128:(h + t + 1) * 128], ident[:, :]),
                            free, k)
                    got.append((h, n4, b, tp))
                crel["xc"] = tp
                if which == 2:
                    for h, n4, b, tp in got:
                        k = act(lambda e, h=h, n4=n4, b=b, m=m: e.activation(
                            vt[:, h:h + n4, m * 128:(m + 1) * 128],
                            PS[b][:, 0:n4 * 128].rearrange("p (t f) -> p t f", f=128), ACT.Copy, scale=0.5), tp, phase)
                        banks.give(b, k)
                    continue
                for h, n4, b, tp in got:
                    k = act(lambda e, h=h, n4=n4, b=b: e.activation(
                        sq[:, h:h + n4, :], PS[b][:, 0:n4 * 128].rearrange("p (t f) -> p t f", f=128), ACT.Square),
                        tp, crel.get("sq"))
                n2 = NT * 2
                k = dve(lambda e, NT=NT, n2=n2: e.tensor_reduce(
                    nr[:, 0:n2], sq[:, 0:NT, :].rearrange("p t (s f) -> p (t s) f", f=64), AX.X, ALU.add), k)
                crel["sq"] = k
                fac = 1.0 if which else 64.0
                k = dve(lambda e, n2=n2, fac=fac: e.tensor_scalar(nr[:, 0:n2], nr[:, 0:n2], fac, 4 * EPS * fac,
                                                                  ALU.mult, ALU.add), k)
                k = act(lambda e, n2=n2: e.activation(nr[:, 0:n2], nr[:, 0:n2], ACT.Sqrt), k)
                k = dve(lambda e, n2=n2: e.reciprocal(nr[:, 0:n2], nr[:, 0:n2]), k)
                for h, n4, b, tp in got:
                    dst = (kt[:, h:h + n4, m * 128:(m + 1) * 128] if which else qt[:, h:h + n4, :])
                    kk = k
                    for s in range(2):
                        kk = dve(lambda e, h=h, n4=n4, b=b, dst=dst, s=s: e.tensor_tensor(
                            dst[:, :, s * 64:s * 64 + 64],
                            PS[b][:, 0:n4 * 128].rearrange("p (t s f) -> p t s f", s=2, f=64)[:, :, s, :],
                            bc(nr[:, h * 2 + s:(h + n4) * 2:2].unsqueeze(2), [P, n4, 64]), ALU.mult), k,
                            phase, crel.get("qt") if not which else None)
                    banks.give(b, kk)
                for h in range(0, NT, 4):
                    n4 = min(4, NT - h)
                    b, free = banks.take()
                    for t in range(n4):
                        src = kt[:, h + t, m * 128:(m + 1) * 128] if which else qt[:, h + t, :]
                        tp = pe(lambda e, b=b, t=t, src=src: e.transpose(
                            PS[b][:, t * 128:(t + 1) * 128], src, ident[:, :]), free, kk)
                    dstT = (kT if which else qT)[:, m, h * 128:(h + n4) * 128]
                    k = act(lambda e, b=b, n4=n4, dstT=dstT: e.activation(dstT, PS[b][:, 0:n4 * 128], ACT.Copy), tp,
                            phase)
                    banks.give(b, k)
                if not which:
                    crel["qt"] = tp
            done(st, tok)
        t_kv = [act.last(), dve.last(), pe.last()]
        dump("kT", kT, t_kv)
        dump("qT", qT, t_kv)
        dump("vt", vt, t_kv)

        phase = everyone()
        slots = [wring.take() for _ in range(3)]
        wfree = [f for _, f in slots]
        M4 = lambda off: A[:, off:off + 1024].rearrange("p (h f) -> p h f", h=8)
        AT = [M4(i * 1024) for i in range(2)]
        IT = [M4(2048 + i * 1024) for i in range(2)]
        Y = [M4(4096 + i * 1024) for i in range(2)]
        YT = [M4(6144 + i * 1024) for i in range(2)]
        IM = [M4(8192 + i * 1024) for i in range(2)]
        LK = [M4(10240 + i * 1024) for i in range(2)]
        SB = [R3(XT + i * 512, 4, 128) for i in range(2)]
        ub_ = [R3(XT + 1024 + i * 512, 8, 64) for i in range(2)]
        rb_ = [R3(CB + 3072, 8, 64), R3(XT + 2048, 8, 64)]
        sml = R3(CB + 3584, 2, 40)
        for dd in range(2):
            gp(lambda e, dd=dd: e.memset(SB[dd], 0.0), phase)
        t_S = [gp.last(), gp.last()]
        o_tok = [None] * 8
        rel = [{}, {}]
        rows2 = lambda s: slice(64 * s, 64 * s + 64)

        def hv(b):
            return PS[b][:, :].rearrange("p (a f) -> p a f", a=4)

        def each_head(mk, toks, n=128):
            res = []
            for s in range(2):
                b, free = banks.take()
                for j in range(4):
                    l, r = mk(s, j)
                    tok = accumulate(PS[b][:, j * n:(j + 1) * n], [(l, r)], (free, toks))
                res.append((b, tok))
            return res

        def delta_prep(dd, t):
            r = rel[dd]
            g = AB[:, t, dd * 8:dd * 8 + 8]
            be = AB[:, t, 16 + dd * 8:24 + dd * 8]
            sv = sml[:, dd, :]
            b, free = banks.take()
            tok = accumulate(PS[b][:, 0:8], [(cum[:, dd, :], g)], (free, t_ab, t_cum))
            tok = accumulate(PS[b][:, 8:16], [(ones, g)], (t_one,))
            k1 = dve(lambda e, b=b: e.tensor_scalar(sv[:, 0:8], PS[b][:, 0:8], -1.0, None, ALU.mult), tok, r.get("sv"))
            k1 = dve(lambda e, b=b: e.tensor_copy(sv[:, 8:16], PS[b][:, 8:16]), tok)
            k2 = dve(lambda e: e.tensor_tensor(sv[:, 24:32], sv[:, 8:16], sv[:, 0:8], ALU.add), k1)
            banks.give(b, k1)
            k3 = act(lambda e: e.activation(sv[:, 16:24], sv[:, 0:8], ACT.Exp, scale=-1.0), k1, r.get("sv"))
            k3 = act(lambda e: e.activation(sv[:, 24:32], sv[:, 24:32], ACT.Exp), k2)
            k3 = act(lambda e: e.activation(sv[:, 32:40], sv[:, 8:16], ACT.Exp), k1)
            r["svt"] = k3
            G8 = IM[dd]
            kq = dve(lambda e: e.tensor_tensor(G8, bc(g.unsqueeze(2), [P, 8, 128]),
                                               bc(cum[:, dd, :].unsqueeze(1), [P, 8, 128]), ALU.mult),
                     t_ab, t_cum, wfree, r.get("im"))
            E = IT[dd]
            for s in range(2):
                b, free = banks.take()
                gv = G8.rearrange("p (j s) f -> p s j f", s=2)[:, s, :, :]
                tok = accumulate(PS[b][:, :], [(ones, gv), (ident[:, :], bc(neg[:, dd, :].unsqueeze(1), [P, 4, 128]))],
                                 (free, kq, t_neg, t_one))
                for j in range(4):
                    ke = act(lambda e, b=b, s=s, j=j: e.activation(
                        E[:, s * 4 + j, :], hv(b)[:, j, :], ACT.Exp, bias=sv[:, 2 * j + s:2 * j + s + 1]), tok, k1,
                        r.get("it"), wfree)
                banks.give(b, ke)
            ti = t * 128
            kk = each_head(lambda s, j: (kT[rows2(s), j, ti:ti + 128], kT[rows2(s), j, ti:ti + 128]), t_kv)
            for s, (b, tok) in enumerate(kk):
                bev = be.rearrange("p (j s) -> p s j", s=2)[:, s, :]
                k = dve(lambda e, b=b, s=s, bev=bev: e.tensor_tensor(
                    AT[dd][:, s * 4:s * 4 + 4, :], hv(b), bc(bev.unsqueeze(2), [P, 4, 128]), ALU.mult), tok,
                    r.get("at"), wfree)
                banks.give(b, k)
            ka = gp(lambda e: e.tensor_tensor(AT[dd], AT[dd], E, ALU.mult), k, ke)
            if t < 8:
                kq = each_head(lambda s, j: (kT[rows2(s), j, ti:ti + 128], qT[rows2(s), j, ti:ti + 128]), t_kv)
                for s, (b, tok) in enumerate(kq):
                    k = dve(lambda e, b=b, s=s: e.tensor_tensor(
                        IT[dd][:, s * 4:s * 4 + 4, :], hv(b), IT[dd][:, s * 4:s * 4 + 4, :], ALU.mult), tok, ka)
                    banks.give(b, k)
            r["itt"] = k
            k = dve(lambda e: e.tensor_tensor(LK[dd], AT[dd], bc(lv[:, dd, 0, :].unsqueeze(1), [P, 8, 128]), ALU.mult),
                    ka, t_lv, r.get("lk"), wfree)
            k = dve(lambda e: e.scalar_tensor_tensor(
                out=YT[dd], in0=LK[dd], scalar=-1.0, in1=bc(ident[:, :].unsqueeze(1), [P, 8, 128]), op0=ALU.mult,
                op1=ALU.add), k, r.get("yt"), wfree)
            r["yt_t"] = [k]
            ks = []
            for s in range(2):
                b, free = banks.take()
                for j in range(4):
                    tok = pe(lambda e, b=b, s=s, j=j: e.transpose(hv(b)[:, j, :], YT[dd][:, s * 4 + j, :], ident[:, :]),
                             free, k)
                kk = act(lambda e, b=b, s=s: e.activation(Y[dd][:, s * 4:s * 4 + 4, :], hv(b), ACT.Copy), tok,
                         r.get("y"), wfree)
                banks.give(b, kk)
                ks.append(kk)
            r["y_t"] = ks
            r["lk"] = r["at_t"] = k

        def level_mask(dd, lev):
            r = rel[dd]
            k = gp(lambda e: e.tensor_tensor(LK[dd], AT[dd], bc(lv[:, dd, lev, :].unsqueeze(1), [P, 8, 128]),
                                             ALU.mult), r["at_t"], r["lk"])
            r["lk_t"] = k

        def level_a(dd, lev):
            r = rel[dd]
            res = each_head(lambda s, j: (LK[dd][:, s * 4 + j, :], Y[dd][:, s * 4 + j, :]), [r["lk_t"], r["y_t"]])
            r["lk"] = res[-1][1]
            r["im_t"] = []
            for s, (b, tok) in enumerate(res):
                k = dve(lambda e, b=b, s=s: e.scalar_tensor_tensor(
                    out=IM[dd][:, s * 4:s * 4 + 4, :], in0=hv(b), scalar=-1.0,
                    in1=bc(ident[:, :].unsqueeze(1), [P, 4, 128]), op0=ALU.mult, op1=ALU.add), tok, r.get("im"))
                banks.give(b, k)
                r["im_t"].append(k)

        def level_b(dd, lev):
            r = rel[dd]
            if lev < LEVELS - 1:
                ry = each_head(lambda s, j: (YT[dd][:, s * 4 + j, :], IM[dd][:, s * 4 + j, :]), [r["im_t"], r["yt_t"]])
            rt = each_head(lambda s, j: (IM[dd][:, s * 4 + j, :], YT[dd][:, s * 4 + j, :]), [r["im_t"], r["yt_t"]])
            last = rt[-1][1]
            r["im"] = last
            if lev < LEVELS - 1:
                r["y_t"] = []
                for s, (b, tok) in enumerate(ry):
                    k = act(lambda e, b=b, s=s: e.activation(Y[dd][:, s * 4:s * 4 + 4, :], hv(b), ACT.Copy), tok)
                    banks.give(b, k)
                    r["y_t"].append(k)
            else:
                r["y"] = r["lk"]
            r["yt_t"] = []
            for s, (b, tok) in enumerate(rt):
                k = act(lambda e, b=b, s=s: e.activation(YT[dd][:, s * 4:s * 4 + 4, :], hv(b), ACT.Copy), tok, last)
                banks.give(b, k)
                r["yt_t"].append(k)

        def bcast64(v, shape=(P, 8, 64)):
            return bc(v.unsqueeze(2), list(shape))

        def delta_step(dd, t):
            r = rel[dd]
            be = AB[:, t, 16 + dd * 8:24 + dd * 8]
            sv = sml[:, dd, :]
            ti = t * 128
            St = SB[dd]
            U, Rr = ub_[dd], rb_[dd]
            p3 = lambda b: PS[b][:, :].rearrange("p (h f) -> p h f", h=8)
            b, free = banks.take()
            for j in range(4):
                tok = accumulate(PS[b][:, j * 128:(j + 1) * 128], [(kT[:, j, ti:ti + 128], St[:, j, :])],
                                 (free, t_S[dd], t_kv))
            k = dve(lambda e, b=b: e.tensor_tensor(Rr, p3(b), bcast64(sv[:, 16:24]), ALU.mult), tok, r["svt"],
                    r.get("r"))
            banks.give(b, k)
            k = dve(lambda e: e.tensor_tensor(Rr, vt[:, t, :].rearrange("p (h f) -> p h f", h=8), Rr, ALU.subtract), k)
            b, free = banks.take()
            for h in range(8):
                i = (h % 2) * 4 + h // 2
                tok = accumulate(PS[b][:, h * 64:(h + 1) * 64], [(YT[dd][:, i, :], Rr[:, h, :])], (free, k, r["yt_t"]))
            r["yt"] = r["r"] = tok
            ku = dve(lambda e, b=b: e.tensor_tensor(U, p3(b), bcast64(be), ALU.mult), tok, r.get("u"))
            banks.give(b, ku)
            kr = dve(lambda e: e.tensor_tensor(Rr, U, bcast64(sv[:, 24:32]), ALU.mult), ku, tok)
            if t < 8:
                b1, free = banks.take()
                for j in range(4):
                    tq = accumulate(PS[b1][:, j * 128:(j + 1) * 128], [(qT[:, j, ti:ti + 128], St[:, j, :])],
                                    (free, t_kv, t_S[dd]))
                b2, free = banks.take()
                for h in range(8):
                    i = (h % 2) * 4 + h // 2
                    to = accumulate(PS[b2][:, h * 64:(h + 1) * 64], [(IT[dd][:, i, :], U[:, h, :])],
                                    (free, ku, r["itt"]))
                r["it"] = r["u"] = to
            b, free = banks.take()
            for j in range(4):
                tok = accumulate(PS[b][:, j * 128:(j + 1) * 128],
                                 [(kt[:, t, j * 128:(j + 1) * 128], Rr[:, 2 * j:2 * j + 2, :])], (free, kr))
            r["r"] = tok
            if t >= 8:
                r["u"] = kr
                r["it"] = r["at_t"]
            p4 = lambda b, s: PS[b][rows2(s), :].rearrange("p (j s f) -> p j s f", j=4, s=2)[:, :, s, :]
            for s in range(2):
                gl = sv[rows2(s), 32:40].rearrange("p (j s) -> p s j", s=2)[:, s, :]
                Sv = St[rows2(s), :, s * 64:s * 64 + 64]
                k = dve(lambda e, gl=gl, Sv=Sv: e.tensor_tensor(Sv, Sv, bcast64(gl, (64, 4, 64)), ALU.mult), tok,
                        r["svt"])
                k = dve(lambda e, Sv=Sv, b=b, s=s: e.tensor_tensor(Sv, Sv, p4(b, s), ALU.add), k)
            banks.give(b, k)
            t_S[dd] = k
            if t < 8:
                Ot = O[:, t, :].rearrange("p (h f) -> p h f", h=8)
                k = dve(lambda e: e.tensor_tensor(Rr, p3(b1), bcast64(sv[:, 16:24]), ALU.mult), tq, r["r"])
                banks.give(b1, k)
                k2 = dve(lambda e: e.tensor_tensor(Rr, Rr, p3(b2), ALU.add), k, to)
                banks.give(b2, k2)
                if o_tok[t] is None:
                    k3 = gp(lambda e: e.tensor_copy(Ot, Rr), k2, phase)
                else:
                    k3 = gp(lambda e: e.tensor_tensor(Ot, Ot, Rr, ALU.add), k2, o_tok[t])
                o_tok[t] = k3
                r["r"] = k3
            r["sv"] = [dve.last(), r["svt"]]
            r["at"] = r["at_t"]

        orders = [[8, 9] + list(range(8)), [9, 8] + list(range(7, -1, -1))]
        for step in range(10):
            for dd in range(2):
                delta_prep(dd, orders[dd][step])
            for lev in range(1, LEVELS):
                for dd in range(2):
                    level_mask(dd, lev)
                for dd in range(2):
                    level_a(dd, lev)
                for dd in range(2):
                    level_b(dd, lev)
                    if lev == LEVELS - 1:
                        rel[dd]["at_t"] = gp.last()
            for dd in range(2):
                delta_step(dd, orders[dd][step])
        t_o = gp.last()
        dump("o", O, t_o)
        t_d = everyone()
        for s, _ in slots:
            wring.give(s, t_d)

        phase = everyone()
        aq = R3(F0, 4, 1024)
        ak = R(F0 + 4096, 1280)
        av = R3(F0 + 5376, 10, 128)
        rope = R3(F0 + 6656, 8, 128)
        gqk = R(F0 + 7680, 640)
        wn = R(F0 + 8320, 384)
        sk = R(F0 + 8704, 8)
        t_rope = load(rope, d["rope"], phase)
        t_gqk = load(gqk, d["rows"][:, ROW["qk"][0]:ROW["qk"][0] + 640], phase)
        t_wn = load(wn, d["wn"], phase)
        t_sk = load(sk, d["rows"][:, ROW["sink"][0]:ROW["sink"][0] + 8], phase)
        T1 = F0 + 8720
        zb = [R(T1 + i * 640, 640) for i in range(2)]
        z2 = [R(T1 + 1280 + i * 640, 640) for i in range(2)]
        z3 = [R(T1 + 2560 + i * 640, 640) for i in range(2)]
        zs = [R(T1 + 3840 + i * 16, 16) for i in range(2)]
        s1 = strip(w2[:, 0:512], 8, 512)
        s2 = strip(w2[:, 512:768], 8, 256)
        zr = [{}, {}]

        def qkv_in(t):
            r = zr[t % 2]
            z = zb[t % 2]
            r["in"] = []
            if t < 8:
                dense_tm(s1, hlhs, [t], 512, lambda t_, o, tok: act(
                    lambda e: e.activation(z[:, 0:512], o, ACT.Copy), tok, r.get("z"), phase), t_h)

            def ev(t_, o, tok):
                act(lambda e: e.activation(z[:, 512:640], o[:, 0:128], ACT.Copy), tok, r.get("z"), phase)
                return act(lambda e: e.activation(av[:, t, :], o[:, 128:256], ACT.Copy), tok, phase)
            dense_tm(s2, hlhs, [t], 256, ev, t_h)
            r["in"] = act.last()

        def qkv_norm(t):
            r = zr[t % 2]
            z, q2, q3, ss = zb[t % 2], z2[t % 2], z3[t % 2], zs[t % 2]
            c0 = 0 if t < 8 else 512
            nh = 10 if t < 8 else 2
            zz, a2, a3, gg = z[:, c0:640], q2[:, c0:640], q3[:, c0:640], gqk[:, c0:640]
            v3 = lambda a: a.rearrange("p (h f) -> p h f", f=64)
            k = dve(lambda e: e.tensor_tensor(a2, zz, zz, ALU.mult), r["in"], r.get("z2"), phase)
            k = dve(lambda e: e.tensor_reduce(ss[:, 0:nh], v3(a2), AX.X, ALU.add), k, r.get("ss"), phase)
            k = dve(lambda e: e.tensor_scalar(ss[:, 0:nh], ss[:, 0:nh], 1.0 / 64, EPS, ALU.mult, ALU.add), k)
            k = act(lambda e: e.activation(ss[:, 0:nh], ss[:, 0:nh], ACT.Sqrt), k)
            k = dve(lambda e: e.reciprocal(ss[:, 0:nh], ss[:, 0:nh]), k)
            k = dve(lambda e: e.tensor_tensor(v3(zz), v3(zz), bc(ss[:, 0:nh].unsqueeze(2), [P, nh, 64]), ALU.mult), k)
            r["ss"] = k
            k = dve(lambda e: e.tensor_tensor(zz, zz, gg, ALU.mult), k, t_gqk)
            if t < 8:
                cs, sn = rope[:, t, 0:64], rope[:, t, 64:128]
                ka = dve(lambda e: e.tensor_tensor(v3(a2), v3(zz), bc(cs.unsqueeze(1), [P, nh, 64]), ALU.mult), k,
                         t_rope)
                v5 = lambda a: a.rearrange("p (h g s f) -> p h g s f", g=2, s=2, f=16)
                sn5 = sn.rearrange("p (g s f) -> p g s f", g=2, s=2)
                for g in range(2):
                    for s in range(2):
                        kb = dve(lambda e, g=g, s=s: e.tensor_tensor(
                            v5(a3)[:, :, g, s, :], v5(zz)[:, :, g, 1 - s, :],
                            bc(sn5[:, g, s, :].unsqueeze(1), [P, 10, 16]), ALU.mult), k, r.get("z3"), t_rope, phase)
                k = dve(lambda e: e.tensor_tensor(zz, a2, a3, ALU.add), ka, kb)
            r["z2"] = r["z3"] = k
            b, free = banks.take()
            if t < 8:
                qp = q2[:, 0:512].rearrange("p (j s f) -> p j s f", j=4, s=2)
                for s in range(2):
                    kp = dve(lambda e, s=s: e.tensor_copy(
                        qp[:, :, s, :], z[:, s * 256:(s + 1) * 256].rearrange("p (j f) -> p j f", f=64)), k)
                for j in range(4):
                    tp = pe(lambda e, j=j: e.transpose(PS[b][:, j * 128:(j + 1) * 128],
                                                       q2[:, j * 128:(j + 1) * 128], ident[:, :]), free, kp)
                ke = act(lambda e: e.activation(aq[:, :, t * 128:(t + 1) * 128], hv(b), ACT.Copy), tp, phase)
                banks.give(b, ke)
                b, free = banks.take()
                r["z2"] = tp
            tp = pe(lambda e: e.transpose(PS[b][:, 0:128], z[:, 512:640], ident[:, :]), free, k)
            ke = act(lambda e: e.activation(ak[:, t * 128:(t + 1) * 128], PS[b][:, 0:128], ACT.Copy), tp, phase)
            banks.give(b, ke)
            r["z"] = tp

        pipeline(10, [qkv_in, qkv_norm], [0, 1])
        done(s1, pe.last())
        done(s2, pe.last())
        t_q = [act.last()]
        dump("aq", aq, t_q)
        dump("ak", ak, t_q)

        T2 = T1 + 3872
        sc_ = Pool_([R(T2 + i * 640, 640) for i in range(3)])
        pp_ = Pool_([R(T1 + i * 640, 640) for i in range(3)])
        pT_ = Pool_([R3(T1 + 1920 + i * 640, 5, 128) for i in range(3)])
        phase = everyone()
        su = {}
        wst = ctx.enter_context(nc.sbuf_tensor("wst", [P, 8, 4], F32))

        def unit(i):
            n, r = divmod(i, 8)
            j, s = divmod(r, 2)
            return n, j, s, j + 4 * s

        def watt_scores(i):
            n, j, s, h = unit(i)
            lo, hi = max(n - 1, 0), min(n + 2, 8)
            nl = (hi - lo) * 128
            m0 = (lo - (n - 1)) * 128
            q = aq[rows2(s), j, n * 128:(n + 1) * 128]
            b1, f1 = banks.take()
            ta = accumulate(PS[b1][:, 0:nl], [(q, ak[rows2(s), lo * 128:hi * 128])], (f1, t_q))
            b2, f2 = banks.take()
            tb = accumulate(PS[b2][:, 0:256], [(q, ak[rows2(s), 1024:1280])], (f2,))
            c = wst[:, i % 8, :]
            z, fz = sc_.take()
            k = dve(lambda e: e.scalar_tensor_tensor(out=z[:, 0:nl], in0=PS[b1][:, 0:nl], scalar=0.125,
                                                     in1=wn[:, m0:m0 + nl], op0=ALU.mult, op1=ALU.add), ta, fz, t_wn,
                    phase)
            banks.give(b1, k)
            kb = dve(lambda e: e.tensor_scalar(z[:, nl:nl + 256], PS[b2][:, 0:256], 0.125, None, ALU.mult), tb, fz)
            banks.give(b2, kb)
            k = dve(lambda e: e.tensor_reduce(c[:, 0:1], z[:, 0:nl + 256], AX.X, ALU.max), kb, k)
            k = dve(lambda e: e.tensor_scalar(c[:, 0:1], c[:, 0:1], sk[:, h:h + 1], -1.0, ALU.max, ALU.mult), k, t_sk)
            p, fp = pp_.take()
            ke = act(lambda e: e.activation(p[:, 0:nl + 256], z[:, 0:nl + 256], ACT.Exp, bias=c[:, 0:1],
                                            accum_out=c[:, 1:2]), k, fp, phase)
            sc_.give(z, ke)
            kf = act(lambda e: e.activation(c[:, 2:3], sk[:, h:h + 1], ACT.Exp, bias=c[:, 0:1]), k)
            k = dve(lambda e: e.tensor_tensor(c[:, 1:2], c[:, 1:2], c[:, 2:3], ALU.add), kf, ke)
            k = dve(lambda e: e.reciprocal(c[:, 3:4], c[:, 1:2]), k)
            k = gp(lambda e: e.tensor_scalar(p[:, 0:nl + 256], p[:, 0:nl + 256], c[:, 3:4], None, ALU.mult), k)
            su[i] = (p, k, lo, hi)

        def watt_tr(i):
            p, k, lo, hi = su[i]
            nt = hi - lo + 2
            q, fq = pT_.take()
            for c0 in range(0, nt, 4):
                n4 = min(4, nt - c0)
                b, free = banks.take()
                for c in range(n4):
                    tp = pe(lambda e, b=b, c=c, c0=c0: e.transpose(
                        PS[b][:, c * 128:(c + 1) * 128], p[:, (c0 + c) * 128:(c0 + c + 1) * 128], ident[:, :]), free, k)
                ke = act(lambda e, b=b, n4=n4, c0=c0: e.activation(
                    q[:, c0:c0 + n4, :], PS[b][:, 0:n4 * 128].rearrange("p (a f) -> p a f", f=128), ACT.Copy), tp, fq)
                banks.give(b, ke)
            pp_.give(p, tp)
            su[i] = (q, ke, lo, hi)

        def watt_pv(i):
            n, j, s, h = unit(i)
            q, ke, lo, hi = su.pop(i)
            tl = list(range(lo, hi)) + [8, 9]
            if s == 0:
                su["b"] = banks.take()
            b, free = su["b"]
            tok = accumulate(PS[b][64 * s:64 * s + 64, 0:128],
                             [(av[:, t, s * 64:s * 64 + 64], q[:, x, :]) for x, t in enumerate(tl)], (free, ke))
            pT_.give(q, tok)
            if s == 1:
                k = dve(lambda e: e.tensor_copy(aq[:, j, n * 128:(n + 1) * 128], PS[b][:, 0:128]), tok)
                banks.give(b, k)

        pipeline(64, [watt_scores, watt_tr, watt_pv], [0, 1, 2])
        t_ya = dve.last()
        dump("ya2", aq, t_ya)

        phase = everyone()
        yd = R3(T1, 4, 1024)
        zz_ = [R(T1 + 4096 + i * 512, 512) for i in range(2)]
        th2 = [R(T1 + 5120 + i * 512, 512) for i in range(2)]
        dn = R(T1 + 6144, 512)
        t_dn = load(dn, d["rows"][:, ROW["dn"][0]:ROW["dn"][0] + 512], phase)
        ss8 = sm[:, 0:64].rearrange("p (t h) -> p t h", h=8)
        v3 = lambda a: a.rearrange("p (h f) -> p h f", f=64)
        for t in range(8):
            q2 = th2[t % 2]
            k = dve(lambda e, t=t, q2=q2: e.tensor_tensor(q2, O[:, t, :], O[:, t, :], ALU.mult), t_o, phase)
            k = dve(lambda e, t=t, q2=q2: e.tensor_reduce(ss8[:, t, :], v3(q2), AX.X, ALU.add), k)
        k = dve(lambda e: e.tensor_scalar(sm[:, 0:64], sm[:, 0:64], 1.0 / 64, EPS, ALU.mult, ALU.add), k)
        k = act(lambda e: e.activation(sm[:, 0:64], sm[:, 0:64], ACT.Sqrt), k)
        t_ss = dve(lambda e: e.reciprocal(sm[:, 0:64], sm[:, 0:64]), k)
        st = strip(w2[:, 2304:2816], 8, 512)
        zrel = [t_ss, t_ss]

        def ev_z(t, o, tok):
            z, q2 = zz_[t % 2], th2[t % 2]
            ka = act(lambda e: e.activation(q2, o, ACT.Tanh, scale=0.5), tok, zrel[t % 2], phase)
            k = dve(lambda e: e.scalar_tensor_tensor(out=z, in0=q2, scalar=1.0, in1=o, op0=ALU.add, op1=ALU.mult), ka,
                    zrel[t % 2])
            free_o = k
            k = dve(lambda e: e.tensor_tensor(v3(q2), v3(O[:, t, :]), bc(ss8[:, t, :].unsqueeze(2), [P, 8, 64]),
                                              ALU.mult), k, t_ss)
            k = dve(lambda e: e.tensor_tensor(q2, q2, dn, ALU.mult), k, t_dn)
            k = dve(lambda e: e.scalar_tensor_tensor(out=z, in0=z, scalar=0.5, in1=q2, op0=ALU.mult, op1=ALU.mult), k)
            b, free = banks.take()
            for j in range(4):
                tp = pe(lambda e, j=j: e.transpose(PS[b][:, j * 128:(j + 1) * 128], z[:, j * 128:(j + 1) * 128],
                                                   ident[:, :]), free, k)
            zrel[t % 2] = tp
            ke = act(lambda e: e.activation(yd[:, :, t * 128:(t + 1) * 128], hv(b), ACT.Copy), tp, phase)
            banks.give(b, ke)
            return free_o
        done(st, dense_tm(st, hlhs, range(8), 512, ev_z, t_h))
        t_yd = act.last()
        dump("yd", yd, t_yd)

        phase = everyone()
        MX = R3(F0 + 16384, 8, 1024)
        tmpx = Pool_([R(CB + i * 512, 512) for i in range(4)])
        slot, free = wring.take()
        wv = R3(W0 + slot * 4096, 4, 1024)
        sp.dma(wv[0:64, :, :], d["w_br_attn_2"][0:256, :].rearrange("(j f) n -> f j n", f=64), wsem[slot], free)
        tw = sp.dma(wv[64:128, :, :], d["w_br_attn_2"][256:512, :].rearrange("(j f) n -> f j n", f=64), wsem[slot])
        wa = (slot, wv, tw)
        sigmoid_mix(MX, None, 4, lambda k, n0, N: aq[:, k, n0:n0 + N],
                    lambda c: w2[:, 2848 + c * 512:3360 + c * 512], None, True, t_ya, tmpx, phase, att=wa)
        done(wa, pe.last())
        wa = strip(d["w_br_dn_2"], 4, 1024)
        k = sigmoid_mix(MX, None, 4, lambda k, n0, N: yd[:, k, n0:n0 + N],
                        lambda c: w2[:, 3872 + c * 512:4384 + c * 512], None, False, t_yd, tmpx, phase, att=wa)
        done(wa, pe.last())
        t_mx = [k, dve.last()]
        phase = everyone()
        dump("mix2", MX, t_mx)
        t_x = sp.dma(X, xs.rearrange("(t p) n -> p t n", p=P), stream("unstash"), phase, t_stash)

        def gate_row(c0, dst, tmp8, *toks):
            for h in range(2):
                b, free = banks.take()
                for q in range(4):
                    k = dve(lambda e, h=h, q=q: e.tensor_scalar(
                        tmp8[:, h * 4 + q, :], ident[:, :], mods[:, c0 + h * 4 + q:c0 + h * 4 + q + 1], None,
                        ALU.mult), *toks)
                tok = accumulate(PS[b][:, :], [(ones1, tmp8[:, h * 4:h * 4 + 4, :])], (free, k, t_one1))
                k = act(lambda e, b=b, h=h: e.activation(dst[:, h * 512:(h + 1) * 512], PS[b][:, :], ACT.Copy), tok,
                        *toks)
                banks.give(b, k)
            return k

        ones1 = R(CB + 3072, 128)
        t_one1 = gp(lambda e: e.memset(ones1, 1.0), phase)
        G1 = R(F1, 1024)
        t_g = gate_row(16, G1, R3(F1 + 1024, 8, 128), phase)
        tmpx = Pool_([R(CB + i * 512, 512) for i in range(4)])
        w_out_pass(d["w_out_2"], X, MX, t_mx, t_x, gate=(G1, t_g), tmp=tmpx)
        t_x = [gp.last(), t_x]
        dump("x2", X, t_x)

        phase = everyone()
        xn = Pool_([R3(F1, 4, 1024), R3(F1 + 4096, 4, 1024)])
        tk = norm_stats(Xt, 8, rs, R(F2, 1024), [t_x, phase])
        t_h = norm_T(Xt, 8, rs, xn, lambda k: gs[:, 16 + k:17 + k], lambda k: mods[:, 24 + k:25 + k], 0, [tk, phase],
                     phase)
        t_hx[0] = t_h
        phase = everyone()
        G2 = R(CB + 2048, 1024)
        t_g = gate_row(40, G2, R3(F1, 8, 128), phase)
        phase = everyone()
        tmpx = Pool_([R(CB + i * 512, 512) for i in range(4)])
        feed_forward(X, d["w_mlp1_2"], d["w_mlp2_2"], t_h, [t_x, phase], FB, tmp=tmpx, gate=(G2, t_g))
        t_x = dve.last()
        finish(nc, ctx, (pe, dve, act, gp, sp), out, X, t_x, dbg)

def finish(nc, ctx, queues, out, X, t_x, dbg):
    pe, dve, act, gp, sp = queues
    so = [ctx.enter_context(nc.semaphore("store")), 0]
    t = sp.dma(out.rearrange("(t p) n -> p t n", p=P), X, so, t_x)
    sp.wait(t, *[v[1] for v in dbg.values()])
    with nc.Block() as block:
        @block.sync
        def _(e):
            sp.replay(e)

        @block.tensor
        def _(e):
            pe.replay(e)

        @block.vector
        def _(e):
            dve.replay(e)

        @block.scalar
        def _(e):
            act.replay(e)

        @block.gpsimd
        def _(e):
            gp.replay(e)

DIRECT = ["x", "w_in", "w_att_o", "w_rg_a", "w_rg_i", "w_rec_o", "w_out", "w_ff1", "w_ff2", "ctx_2", "w_ada_2",
          "w_in_2", "w_br_attn_2", "w_br_dn_2", "w_out_2", "w_mlp1_2", "w_mlp2_2"]

def layout(inputs):
    a = {k: np.asarray(v) for k, v in inputs.items()}
    got = {n: np.ascontiguousarray(a[n].reshape(a[n].shape[1:])) for n in DIRECT}

    def col(v):
        return v.reshape(-1, 128).T

    b_in = a["b_in"][0]
    cols = {
        "ln1": col(a["ln1_g"][0]), "ln2": col(a["ln2_g"][0]), "bq": col(b_in[0:512]), "bk": col(b_in[512:1024]),
        "bu": col(b_in[1536:2560]), "by": col(b_in[2560:3584]), "bga": col(b_in[3584:4608]),
        "bgr": col(b_in[4608:5632]), "cw": col(a["conv_w"][0]), "cb": col(a["conv_b"][0]),
        "ba": col(a["b_rg_a"][0]), "bi": col(a["b_rg_i"][0]), "lam": col(a["lru_lambda"][0]),
        "c2": np.stack([col(a["c_2"][0]), col(a["c_ctx_2"])], 2).reshape(128, 16), "bada": col(a["b_ada_2"][0]),
        "g1": col(a["g_norm1_2"][0]), "g2": col(a["g_norm2_2"][0]), "cw2": col(a["conv_w_2"][0]),
    }
    got["vecs"] = np.ascontiguousarray(np.concatenate([cols[n] for n in VEC], 1))
    rows = {
        "bv": b_in[1024:1536], "lnf": a["lnf_g"],
        "qk": np.concatenate([np.tile(a["q_norm_g_2"][0], 8), np.tile(a["k_norm_g_2"][0], 2)]),
        "dn": np.tile(a["dn_norm_g_2"][0], 8), "dt": a["dt_bias_2"][0].reshape(-1), "al": a["a_log_2"][0].reshape(-1),
        "sink": a["attn_sink_2"][0],
    }
    row = np.concatenate([rows[n] for n in ROW])
    got["rows"] = np.ascontiguousarray(np.broadcast_to(row[None, :], (128, NROW)))
    q = np.arange(64)
    idx = np.clip(q[None, :] - q[:, None] + 15, 0, 30)
    nb = a["rpb"][0][:, :, idx]
    nb = nb.reshape(4, 2, 15, 64, 64).transpose(1, 3, 0, 2, 4)
    got["nbias"] = np.ascontiguousarray(nb.reshape(128, 4, 960))
    c = shape_constants()
    c["lv"] = c["lv"].reshape(128, 2, LEVELS, 128)
    c["cum"] = c["cum"].reshape(128, 2, 128)
    c["neg"] = c["neg"].reshape(128, 2, 128)
    c["rope"] = c["rope"].reshape(128, 8, 128)
    got.update(c)
    return got

def kernel(**inputs):
    import concourse.bacc as _bacc
    from concourse.bass_utils import run_bass_kernel_spmd as _run

    got = layout(inputs)
    nc = _bacc.Bacc("TRN2", target_bir_lowering=False, num_devices=1)
    arrays, d = {}, {}
    for name, v in got.items():
        arrays["in_" + name] = v
        d[name] = nc.dram_tensor("in_" + name, v.shape, mybir.dt.from_np(v.dtype), kind="ExternalInput").ap()
    d["w_ada"] = d["w_ada_2"]
    out = nc.dram_tensor("out_0", (S, 1024), F32, kind="ExternalOutput").ap()
    build(nc, d, out)
    r = _run(nc, [arrays], core_ids=[0])
    return r.results[0]["out_0"].reshape(1, S, 1024)
```

```python
from contextlib import ExitStack

import numpy as np

import concourse.bass as bass
from concourse import mybir

F32 = mybir.dt.float32
F32R = mybir.dt.float32r
ALU = mybir.AluOpType
ACT = mybir.ActivationFunctionType
AX = mybir.AxisListType
P = 128
S = 1024
CTX = 256
EPS = 1e-6
GC = 0.7978845608028654
VEC = {}
VN = [0]
for _n, _w in [("ln1", 8), ("ln2", 8), ("bq", 4), ("bk", 4), ("bu", 8), ("by", 8), ("bga", 8), ("bgr", 8),
               ("cw", 32), ("cb", 8), ("ba", 16), ("bi", 16), ("lam", 16), ("c2", 16), ("bada", 48),
               ("g1", 8), ("g2", 8), ("cw2", 36)]:
    VEC[_n] = (VN[0], _w)
    VN[0] += _w
NVEC = VN[0]
ROW = {}
RN = [0]
for _n, _w in [("bv", 512), ("lnf", 1024), ("qk", 640), ("dn", 512), ("dt", 16), ("al", 16), ("sink", 8)]:
    ROW[_n] = (RN[0], _w)
    RN[0] += _w
NROW = RN[0]
LEVELS = 7

def shape_constants():
    i = np.arange(128)
    c = {}
    c["ident"] = np.eye(128, dtype=np.float32)
    lv = np.zeros((128, 2, LEVELS, 128), np.float32)
    for k in range(LEVELS):
        m = 1 << k
        same = (i[:, None] // (2 * m)) == (i[None, :] // (2 * m))
        lo = (i // m) % 2 == 0
        hi = ~lo
        lv[:, 0, k, :] = same & lo[:, None] & hi[None, :]
        lv[:, 1, k, :] = same & hi[:, None] & lo[None, :]
    c["lv"] = lv.reshape(128, -1)
    cum = np.zeros((128, 2, 128), np.float32)
    cum[:, 0, :] = i[:, None] <= i[None, :]
    cum[:, 1, :] = i[:, None] >= i[None, :]
    c["cum"] = cum.reshape(128, -1)
    neg = np.where(cum > 0, 0.0, -1e30).astype(np.float32)
    c["neg"] = neg.reshape(128, -1)
    wn = np.zeros((128, 3, 128), np.float32)
    wn[:, 0, :] = np.where(i[None, :] >= i[:, None], 0.0, -1e30)
    wn[:, 2, :] = np.where(i[None, :] <= i[:, None], 0.0, -1e30)
    c["wn"] = wn.reshape(128, -1)
    pos = np.arange(S)
    fr = (np.float32(10000.0) ** (-np.arange(16, dtype=np.float32) / np.float32(16))).astype(np.float32)
    ar = (pos // 64).astype(np.float32)[:, None] * fr
    ac = (pos % 64).astype(np.float32)[:, None] * fr
    cos = np.concatenate([np.cos(ar), np.cos(ar), np.cos(ac), np.cos(ac)], 1)
    sin = np.concatenate([-np.sin(ar), np.sin(ar), -np.sin(ac), np.sin(ac)], 1)
    rope = np.concatenate([cos, sin], 1).astype(np.float32)
    c["rope"] = np.ascontiguousarray(rope.reshape(8, 128, 128).transpose(1, 0, 2)).reshape(128, -1)
    q = np.arange(64)
    ws = np.clip(q - 8, 0, 48)
    k = np.arange(64)
    nm = np.where((k[None, :] >= ws[:, None]) & (k[None, :] < ws[:, None] + 16), 0.0, -1e30).astype(np.float32)
    c["nm"] = np.concatenate([nm, nm], 0)
    return c

CONST = [("ident", 128), ("lv", 2 * LEVELS * 128), ("cum", 256), ("neg", 256), ("wn", 384), ("rope", 1024), ("nm", 64)]

class Said:

    def matmul(self, *a, **k):
        return lambda e: e.matmul(*a, **k)

    def transpose(self, *a, **k):
        return lambda e: e.transpose(*a, **k)

    def activation(self, *a, **k):
        return lambda e: e.activation(*a, **k)

    def tensor_tensor(self, *a, **k):
        return lambda e: e.tensor_tensor(*a, **k)

    def tensor_scalar(self, *a, **k):
        return lambda e: e.tensor_scalar(*a, **k)

    def scalar_tensor_tensor(self, *a, **k):
        return lambda e: e.scalar_tensor_tensor(*a, **k)

    def tensor_tensor_scan(self, *a, **k):
        return lambda e: e.tensor_tensor_scan(*a, **k)

    def tensor_copy(self, *a, **k):
        return lambda e: e.tensor_copy(*a, **k)

    def tensor_reduce(self, *a, **k):
        return lambda e: e.tensor_reduce(*a, **k)

    def reciprocal(self, *a, **k):
        return lambda e: e.reciprocal(*a, **k)

    def memset(self, *a, **k):
        return lambda e: e.memset(*a, **k)

SAID = Said()

class Queue:

    def __init__(self, nc, ctx, name):
        self.sem = ctx.enter_context(nc.semaphore("s_" + name))
        self.items, self.n, self.seen = [], 0, {}

    def wait(self, *toks):
        for t in toks:
            if t is None:
                continue
            if isinstance(t, list):
                self.wait(*t)
                continue
            sem, val = t
            if self.seen.get(id(sem), 0) < val:
                self.seen[id(sem)] = val
                self.items.append(lambda e, sem=sem, val=val: e.wait_ge(sem, val))

    def __call__(self, fn, *toks):
        self.wait(*toks)
        self.n += 1
        issue = fn(SAID)
        self.items.append(lambda e: issue(e).then_inc(self.sem, 1))
        return (self.sem, self.n)

    def quiet(self, fn, *toks):
        self.wait(*toks)
        self.items.append(fn(SAID))

    def dma(self, out, in_, stream, *toks):
        self.wait(*toks)
        stream[1] += 16
        sem, val = stream
        self.items.append(lambda e: e.dma_start(out, in_).then_inc(sem, 16))
        return (sem, val)

    def last(self):
        return (self.sem, self.n) if self.n else None

    def replay(self, e):
        for it in self.items:
            it(e)

class Pool_:

    def __init__(self, places):
        self.free = [(p, None) for p in places]

    def take(self):
        return self.free.pop(0)

    def give(self, place, *toks):
        self.free.append((place, list(toks)))

def pipeline(n, stages, lags=None):
    lags = lags or list(range(len(stages)))
    for i in range(n + max(lags)):
        for st, lag in zip(stages, lags):
            if 0 <= i - lag < n:
                st(i - lag)

def build(nc, d, out, dbg=None, upto=99):
    dbg = dbg or {}
    ctx = ExitStack()
    with ctx:
        def stream(name):
            return [ctx.enter_context(nc.semaphore(name)), 0]

        pe, dve, act, gp, sp = (Queue(nc, ctx, n) for n in ("pe", "dve", "act", "gp", "sp"))
        with nc.sbuf_tensor("arena", [P, 52480], F32) as A:
            pass
        with nc.sbuf_tensor("below", [P, 16384], F32), nc.sbuf_tensor("raws", [P, 4096], F32) as RAW, \
                nc.sbuf_tensor("tmps", [P, 2048], F32) as TMP:
            pass
        RR = ctx.enter_context(nc.sbuf_tensor("halves", [P, 52480], F32R))
        ident = ctx.enter_context(nc.sbuf_tensor("identm", [P, 128], F32))
        vec = ctx.enter_context(nc.sbuf_tensor("vec", [P, NVEC], F32))
        sm = ctx.enter_context(nc.sbuf_tensor("sm", [P, 64], F32))
        PS = [ctx.enter_context(nc.psum_tensor(f"ps{i}", [P, 512], F32)) for i in range(8)]
        banks = Pool_(range(8))
        W0, HT0, F0, CB = 0, 12288, 22528, 48640
        F1, F2 = F0 + 8192, F0 + 16384
        hs = nc.dram_tensor("h_stash", [P, 10240], F32, kind="Internal").ap()
        xs = nc.dram_tensor("x_stash", [S, 1024], F32, kind="Internal").ap()

        def R(off, n):
            return A[:, off:off + n]

        def R3(off, a, b):
            return A[:, off:off + a * b].rearrange("p (a b) -> p a b", a=a)

        def Q3(off, a, b):
            return RR[:, off:off + a * b].rearrange("p (a b) -> p a b", a=a)

        def V(name, j, n=1):
            o = VEC[name][0] + j
            return vec[:, o:o + n]

        def everyone():
            return [q.last() for q in (pe, dve, act, gp)]

        def bc(ap, shape):
            return ap.to_broadcast(shape)

        ldvec = stream("ldvec")
        t_vec = sp.dma(vec[:, :], d["vecs"], ldvec)
        t_id = sp.dma(ident[:, :], d["ident"], stream("ldid"))
        misc = [stream(f"misc{i}") for i in range(24)]

        def load(dst, src, *toks, q=None):
            return (q or sp).dma(dst, src, misc.pop(0), *toks)

        def dump(name, ap, *toks):
            if name in dbg:
                dbg[name][1] = sp.dma(dbg[name][0], ap, stream("dbg" + name), *toks)
                for q in (pe, dve, act, gp):
                    q.wait(dbg[name][1])

        wring = Pool_(range(3))
        wsem = [stream(f"w{i}") for i in range(3)]

        def strip(src, kt, n, *toks):
            slot, free = wring.take()
            view = R3(W0 + slot * 4096, kt, n)
            tok = sp.dma(view, src.rearrange("(k p) n -> p k n", p=P), wsem[slot], free, *toks)
            return slot, view, tok

        HT = R3(HT0, 8, 1280)

        def accumulate(out_ap, pairs, toks, start=True, stop=True):
            n = len(pairs)
            for i, (l, r) in enumerate(pairs):
                def mm(e, l=l, r=r, i=i):
                    return e.matmul(out_ap, l, r, start=start and i == 0, stop=stop and i == n - 1)
                if i < n - 1:
                    pe.quiet(mm, *(toks if i == 0 else ()))
                else:
                    tok = pe(mm, *(toks if i == 0 else ()))
            return tok

        def dense_fm(st, rhs, pieces, evac, tok_r, kt=8, mts=None):
            slot, w, tw = st
            for m in (range(4) if mts is None else mts):
                for n0, N in pieces:
                    b, free = banks.take()
                    o = PS[b][:, 0:N]
                    tok = accumulate(o, [(w[:, k, m * 128:(m + 1) * 128], rhs(k, n0, N)) for k in range(kt)],
                                     (free, tw, tok_r))
                    banks.give(b, evac(m, n0, N, o, tok))
            return tok

        def dense_tm(st, lhs, tiles, N, evac, tok_r, c0=0, kt=8):
            slot, w, tw = st
            for t in tiles:
                b, free = banks.take()
                o = PS[b][:, 0:N]
                tok = accumulate(o, [(lhs(k, t), w[:, k, c0:c0 + N]) for k in range(kt)], (free, tw, tok_r))
                banks.give(b, evac(t, o, tok))
            return tok

        def done(st, tok):
            wring.give(st[0], tok)

        hrhs = lambda k, n0, N: HT[:, k, n0:n0 + N]
        hlhs = lambda k, t: HT[:, k, t * 128:(t + 1) * 128]
        HALVES = [(0, 512), (512, 512)]

        def norm_stats(X, nt, ss, junk, tok_x, width=1024):
            for t in range(nt):
                tk = act(lambda e, t=t: e.activation(junk, X(t), ACT.Square, accum_out=ss[:, t:t + 1]),
                         tok_x, act.last())
            tk = dve(lambda e: e.tensor_scalar(ss, ss, 1.0 / width, EPS, ALU.mult, ALU.add), tk)
            tk = act(lambda e: e.activation(ss, ss, ACT.Sqrt), tk)
            return dve(lambda e: e.reciprocal(ss, ss), tk)

        def norm_T3(X, ss, xn, gcol, scol, hl, tmp, tok, tok_ht):
            for h in range(0, 8, 4):
                place, free = xn.take()
                for t in range(4):
                    tn = dve(lambda e, t=t: e.tensor_scalar(
                        place[:, t, :], X(h + t), ss[:, h + t:h + t + 1], None, ALU.mult), tok, free)
                for k in range(8):
                    b, fb = banks.take()
                    for t in range(4):
                        tp = pe(lambda e, t=t: e.transpose(
                            PS[b][:, t * 128:(t + 1) * 128], place[:, t, k * 128:(k + 1) * 128], ident[:, :]),
                            fb, tn, t_id)
                    tt, ft = tmp.take()
                    te = act(lambda e: e.activation(tt, PS[b][:, :], ACT.Identity, scale=gcol(k),
                                                    bias=scol(k) if scol else 0.0), tp, ft)
                    banks.give(b, te)
                    tmp.give(tt, split(tt, hl[0][:, k, h * 128:h * 128 + 512], hl[1][:, k, h * 128:h * 128 + 512],
                                       te, tok_ht))
                xn.give(place, tp)
            return [act.last(), dve.last()]

        def split(src, hi, lo, *toks):
            k = act(lambda e: e.activation(hi, src, ACT.Copy), *toks)
            return dve(lambda e: e.tensor_tensor(lo, src, hi.bitcast(F32), ALU.subtract), k)

        def norm_T(X, nt, ss, xn, gcol, scol, h0, tok, tok_ht):
            toks = []
            for h in range(0, nt, 4):
                n4 = min(4, nt - h)
                place, free = xn.take()
                for t in range(n4):
                    tn = dve(lambda e, t=t, h=h, place=place: e.tensor_scalar(
                        place[:, t, :], X(h + t), ss[:, h + t:h + t + 1], None, ALU.mult), tok, free)
                for k in range(8):
                    b, fb = banks.take()
                    for t in range(n4):
                        tp = pe(lambda e, b=b, t=t, k=k, place=place: e.transpose(
                            PS[b][:, t * 128:(t + 1) * 128], place[:, t, k * 128:(k + 1) * 128], ident[:, :]),
                            fb, tn, t_id)
                    dst = HT[:, k, h0 + h * 128:h0 + (h + n4) * 128]
                    if k % 2:
                        te = dve(lambda e, b=b, k=k, dst=dst, n4=n4: e.tensor_scalar(
                            dst, PS[b][:, 0:n4 * 128], gcol(k), scol(k) if scol else None, ALU.mult,
                            ALU.add if scol else ALU.bypass), tp, tok_ht)
                    else:
                        te = act(lambda e, b=b, k=k, dst=dst, n4=n4: e.activation(
                            dst, PS[b][:, 0:n4 * 128], ACT.Identity, scale=gcol(k),
                            bias=scol(k) if scol else 0.0), tp, tok_ht)
                    banks.give(b, te)
                    toks.append(te)
                xn.give(place, tp)
            return toks[-2:]

        X = R3(F0, 8, 1024)
        Xt = lambda t: X[:, t, :]
        t_x = sp.dma(X, d["x"].rearrange("(t p) n -> p t n", p=P), stream("ldx"))
        xn = Pool_([R3(F1, 4, 1024), R3(F1 + 4096, 4, 1024)])
        rs = sm[:, 0:8]
        tk = norm_stats(Xt, 8, rs, R(F2, 1024), t_x)
        t_h = norm_T(Xt, 8, rs, xn, lambda k: V("ln1", k), None, 0, [tk, t_vec], None)
        dump("h1", HT[:, :, 0:1024], t_h)

        w_in = d["w_in"]
        QB = A[:, F0:F0 + 8192].rearrange("p (j r s q) -> p j r s q", j=4, r=16, s=2)
        KT = R3(F1, 4, 1024)
        VT = R3(F1 + 4096, 8, 512)
        VS = R3(F2, 7, 512)
        BI = R3(CB, 4, 960)
        phase = everyone()
        tz = gp(lambda e: e.memset(R(F0, 8192), 0.0), phase)
        nm = R(F2 + 3584, 64)
        bvr = R(F2 + 3648, 512)
        t_nm = load(nm, d["nm"], phase)
        t_bv = load(bvr, d["rows"][:, ROW["bv"][0]:ROW["bv"][0] + 512], phase)
        t_bi = load(BI, d["nbias"], phase)
        for j in range(4):
            t_bi2 = gp(lambda e, j=j: e.tensor_tensor(
                BI[:, j, :].rearrange("p (a k) -> p a k", k=64), BI[:, j, :].rearrange("p (a k) -> p a k", k=64),
                bc(nm.unsqueeze(1), [P, 15, 64]), ALU.add), t_bi, t_nm)

        def ev_q(m, n0, N, o, tok):
            for s in range(2):
                rows = slice(64 * s, 64 * s + 64)
                tk = dve(lambda e, s=s, rows=rows: e.tensor_scalar(
                    QB[rows, m, n0 // 64:(n0 + N) // 64, s, :], o[rows].rearrange("p (r q) -> p r q", q=64),
                    V("bq", m)[rows], 0.125, ALU.add, ALU.mult), tok, tz)
            return tk

        def ev_k(m, n0, N, o, tok):
            return act(lambda e: e.activation(KT[:, m, n0:n0 + N], o, ACT.Identity, bias=V("bk", m)), tok, phase)

        st = strip(w_in[:, 0:512], 8, 512)
        done(st, dense_fm(st, hrhs, HALVES, ev_q, t_h))
        st = strip(w_in[:, 512:1024], 8, 512)
        done(st, dense_fm(st, hrhs, HALVES, ev_k, t_h))
        st = strip(w_in[:, 1024:1536], 8, 512)
        done(st, dense_tm(st, hlhs, range(8), 512,
                          lambda t, o, tok: dve(lambda e: e.tensor_tensor(VT[:, t, :], o, bvr, ALU.add), tok, t_bv, phase),
                          t_h))
        vsst = stream("vshift")
        tv = dve.last()
        act.dma(VS[0:64, :, :], VT[64:128, 0:7, :], vsst, tv, phase)
        t_vs = act.dma(VS[64:128, :, :], VT[0:64, 1:8, :], vsst)

        T0 = F2 + 4160
        sb = Pool_([R(T0 + i * 512, 512) for i in range(2)])
        pbuf = Pool_([R(T0 + 1024 + i * 512, 512) for i in range(4)])
        ptb = Pool_([R3(T0 + 3072 + i * 512, 4, 128) for i in range(3)])
        st1 = {}
        tqk = [dve.last(), act.last()]
        statn = sm[:, 8:32].rearrange("p (a b) -> p a b", b=3)

        def natt_scores(i):
            r, j = divmod(i, 4)
            start = min(max(r - 4, 0), 8)
            b, free = banks.take()
            tok = accumulate(PS[b][:, :], [(QB[:, j, r, :, :], KT[:, j, start * 64:start * 64 + 512])], (free, tqk))
            off = start - r + 7
            sbt, fs = sb.take()
            tk = dve(lambda e: e.tensor_tensor(sbt, PS[b][:, :], BI[:, j, off * 64:off * 64 + 512], ALU.add),
                     tok, fs, t_bi2)
            banks.give(b, tk)
            c = statn[:, i % 8, :]
            tk = dve(lambda e: e.tensor_reduce(c[:, 0:1], sbt, AX.X, ALU.max, negate=True), tk)
            pt, fp = pbuf.take()
            te = act(lambda e: e.activation(pt, sbt, ACT.Exp, bias=c[:, 0:1], accum_out=c[:, 1:2]), tk, fp)
            sb.give(sbt, te)
            tk = dve(lambda e: e.reciprocal(c[:, 2:3], c[:, 1:2]), te)
            st1[i] = (pt, c, tk, start)

        def natt_scale(i):
            pt, c, tk, start = st1[i]
            tk = gp(lambda e: e.tensor_scalar(pt, pt, c[:, 2:3], None, ALU.mult), tk)
            st1[i] = (pt, tk, start)

        def natt_tr(i):
            pt, tk, start = st1[i]
            b, free = banks.take()
            for c in range(4):
                tp = pe(lambda e, c=c: e.transpose(PS[b][:, c * 128:(c + 1) * 128], pt[:, c * 128:(c + 1) * 128],
                                                   ident[:, :]), tk, free)
            pbuf.give(pt, tp)
            q, fq = ptb.take()
            te = act(lambda e: e.activation(q, PS[b][:, :].rearrange("p (a b) -> p a b", a=4), ACT.Copy), tp, fq)
            banks.give(b, te)
            st1[i] = (q, te, start)

        def natt_pv(i):
            q, te, start = st1.pop(i)
            r, j = divmod(i, 4)
            b, free = banks.take()
            if start % 2:
                vv = [VS[:, start // 2 + c, j * 128:(j + 1) * 128] for c in range(4)]
            else:
                vv = [VT[:, start // 2 + c, j * 128:(j + 1) * 128] for c in range(4)]
            tok = accumulate(PS[b][:, 0:128], [(vv[c], q[:, c, :]) for c in range(4)], (te, free, t_vs))
            ptb.give(q, tok)
            t1 = dve(lambda e: e.tensor_copy(QB[0:64, j, r, 0, :], PS[b][0:64, 0:64]), tok)
            t2 = dve(lambda e: e.tensor_copy(QB[64:128, j, r, 0, :], PS[b][64:128, 64:128]), tok)
            banks.give(b, t2)

        pipeline(64, [natt_scores, natt_scale, natt_tr, natt_pv], [0, 0, 2, 3])
        YA = QB[:, :, :, 0, :]
        dump("yatt", YA, dve.last())
        t_ya = dve.last()

        RC = R3(F1, 8, 1024)
        phase = everyone()
        wrg = stream("wrg")
        hb = ctx.enter_context(nc.sbuf_tensor("hb", [P, 80], F32))
        th = dve(lambda e: e.tensor_scalar(hb[:, 0:32], V("ba", 0, 32), 0.5, None, ALU.mult), phase, t_vec)
        assert VEC["bi"][0] == VEC["ba"][0] + 16
        tk = act(lambda e: e.activation(hb[:, 32:48], V("lam", 0, 16), ACT.Abs), phase, t_vec)
        tk = act(lambda e: e.activation(hb[:, 32:48], hb[:, 32:48], ACT.Exp, scale=-1.0), tk)
        tk = act(lambda e: e.activation(hb[:, 32:48], hb[:, 32:48], ACT.Ln, bias=1.0), tk)
        t2 = dve(lambda e: e.tensor_scalar(hb[:, 48:64], V("lam", 0, 16), -1.0, 0.0, ALU.mult, ALU.max), th)
        t2 = dve(lambda e: e.tensor_tensor(hb[:, 32:48], hb[:, 32:48], hb[:, 48:64], ALU.add), tk, t2)
        t3 = dve(lambda e: e.tensor_scalar(hb[:, 32:48], hb[:, 32:48], 4.0, None, ALU.mult), t2)
        t3 = dve(lambda e: e.tensor_scalar(hb[:, 48:64], hb[:, 32:48], -1.0, None, ALU.mult), t3)
        tk = dve(lambda e: e.tensor_scalar(hb[:, 64:80], V("bga", 0, 16), 0.5, None, ALU.mult), t_vec)
        assert VEC["bgr"][0] == VEC["bga"][0] + 8
        t_hb = dve.last()

        B0 = F2
        ub = [R(B0 + i * 1032, 1028) for i in range(2)]
        rb = B0 + 2064
        uc_, y_, t1_, a_, s_, iu_, hf_ = (R(rb + i * 1024, 1024) for i in range(7))
        ys = [y_.rearrange("p (r q) -> p r q", q=64), QB[:, 0, :, 1, :]]
        t13 = t1_.rearrange("p (r q) -> p r q", q=64)
        hb_ = R(CB, 1024)
        t2_ = R(CB + 1024, 1024)
        gw = [R3(CB + 2048 + i * 512, 4, 128) for i in range(2)]
        gwd = stream("gw0"), stream("gw1")
        tz = None
        for i in range(2):
            tz = gp(lambda e, i=i: e.memset(ub[i][:, 0:2], 0.0), phase)
            tz = gp(lambda e, i=i: e.memset(ub[i][:, 1026:1028], 0.0), phase)
            tz = gp(lambda e, i=i: e.memset(gw[i], 0.0), phase)
        urel = [None, None]
        gwrel = [None, None]
        rsc = {}
        strips = {}

        def rec_in(t):
            c = t // 4
            if t % 4 == 0:
                strips["u"] = strip(w_in[:, 1536 + c * 512:2048 + c * 512], 8, 512)
                strips["y"] = strip(w_in[:, 2560 + c * 512:3072 + c * 512], 8, 512)
            u = ub[t % 2]
            g = gw[t % 2]
            for s in range(2):
                for w, nm_ in enumerate(("w_rg_a", "w_rg_i")):
                    for dd in range(2):
                        tg = act.dma(g[64 * s:64 * s + 64, dd * 2 + w, 64 * s:64 * s + 64],
                                     d[nm_][dd, 2 * t + s, :, :], gwd[t % 2], tz, gwrel[t % 2])
            tok = dense_fm(strips["u"], hrhs, HALVES,
                     lambda m, n0, N, o, tk: act(lambda e: e.activation(
                         u[:, 2 + n0:2 + n0 + N], o, ACT.Identity, bias=V("bu", t)), tk, tz, urel[t % 2], t_hb),
                     t_h, mts=[t % 4])
            tu = act.last()
            tok = dense_fm(strips["y"], hrhs, HALVES,
                           lambda m, n0, N, o, tk: act(lambda e: e.activation(
                               ys[t % 2][:, n0 // 64:(n0 + N) // 64, :], o.rearrange("p (r q) -> p r q", q=64),
                               ACT.Identity, bias=V("by", t)), tk, rsc.get(("y", t % 2)), phase),
                           t_h, mts=[t % 4])
            ty = act.last()
            if t % 4 == 3:
                done(strips["u"], tok)
                done(strips["y"], tok)
            rsc[t] = (tg, tu, ty)

        def rec_tile(t):
            tg, tu, ty = rsc.pop(t)
            u = ub[t % 2]
            g = gw[t % 2]
            cw = lambda j: V("cw", j * 8 + t)
            k1 = dve(lambda e: e.tensor_tensor(t13, ys[t % 2], ys[t % 2], ALU.mult), ty, rsc.get("t1"))
            k1 = dve(lambda e: e.tensor_scalar(t1_, t1_, 0.044715, 1.0, ALU.mult, ALU.add), k1)
            k1 = dve(lambda e: e.tensor_tensor(t13, t13, ys[t % 2], ALU.mult), k1)
            k2 = act(lambda e: e.activation(t1_, t1_, ACT.Tanh, scale=GC), k1)
            k = dve(lambda e: e.tensor_scalar(uc_, u[:, 0:1024], cw(0), V("cb", t), ALU.mult, ALU.add), tu,
                    rsc.get("uc"))
            for j in range(1, 4):
                k = dve(lambda e, j=j: e.scalar_tensor_tensor(out=uc_, in0=u[:, j:j + 1024], scalar=cw(j), in1=uc_,
                                                              op0=ALU.mult, op1=ALU.add), k)
            urel[t % 2] = k
            tuc = k
            k1 = dve(lambda e: e.scalar_tensor_tensor(out=t13, in0=t13, scalar=1.0, in1=ys[t % 2], op0=ALU.add,
                                                      op1=ALU.mult), k2)
            rsc[("y", t % 2)] = k1
            for dd in range(2):
                h = hf_ if dd == 0 else hb_
                for w, (dst, bo) in enumerate(((a_, dd * 8 + t), (iu_, 16 + dd * 8 + t))):
                    for n0, N in HALVES:
                        b, free = banks.take()
                        tok = accumulate(PS[b][:, :], [(g[:, dd * 2 + w, :], uc_[:, n0:n0 + N])], (free, tg, tuc))
                        k = act(lambda e, b=b, dst=dst, bo=bo, n0=n0: e.activation(
                            dst[:, n0:n0 + 512], PS[b][:, :], ACT.Tanh, scale=0.5, bias=hb[:, bo:bo + 1]), tok,
                            rsc.get("a" if w == 0 else "iu"))
                        banks.give(b, k)
                    if w == 0:
                        ka = k
                kp, kn = hb[:, 32 + dd * 8 + t:33 + dd * 8 + t], hb[:, 48 + dd * 8 + t:49 + dd * 8 + t]
                ks = act(lambda e, kp=kp: e.activation(s_, a_, ACT.Tanh, scale=kp, bias=kp), ka, rsc.get("s"))
                ke = act(lambda e, kn=kn: e.activation(a_, a_, ACT.Exp, scale=kn, bias=kn), ks)
                kq = dve(lambda e: e.tensor_tensor(t2_, a_, a_, ALU.mult), ke, rsc.get("t2"))
                kq = dve(lambda e: e.scalar_tensor_tensor(out=s_, in0=t2_, scalar=1.0, in1=s_, op0=ALU.add,
                                                          op1=ALU.mult), kq)
                ks = act(lambda e: e.activation(s_, s_, ACT.Sqrt, scale=0.25), kq)
                ki = dve(lambda e: e.scalar_tensor_tensor(out=iu_, in0=iu_, scalar=1.0, in1=uc_, op0=ALU.add,
                                                          op1=ALU.mult), k)
                ki = dve(lambda e: e.tensor_tensor(iu_, iu_, s_, ALU.mult), ki, ks)
                rsc["s"] = ki
                if dd == 0:
                    kh = dve(lambda e, h=h: e.tensor_tensor_scan(h, a_, iu_, 0.0, ALU.mult, ALU.add), ki, rsc.get("h"))
                else:
                    kh = dve(lambda e, h=h: e.tensor_tensor_scan(h[:, ::-1], a_[:, ::-1], iu_[:, ::-1], 0.0, ALU.mult,
                                                                 ALU.add), ki, rsc.get("h"))
                rsc["a"] = rsc["iu"] = kh
            rsc["t2"] = kq
            rsc["uc"] = kh
            gwrel[t % 2] = tok
            k = dve(lambda e: e.tensor_tensor(hf_, hf_, hb_, ALU.add), kh)
            k = dve(lambda e: e.scalar_tensor_tensor(out=RC[:, t, :], in0=hf_, scalar=0.5, in1=t1_, op0=ALU.mult,
                                                     op1=ALU.mult), k, phase)
            rsc["h"] = rsc["t1"] = k

        pipeline(8, [rec_in, rec_tile], [0, 1])
        t_rc = dve.last()
        dump("rec", RC, t_rc)

        def sigmoid_mix(MX, src_att, kt_att, rhs_att, src_gate, bcol, first, tok_r, tmp, tok_prev, att=None, between=None):
            for c in range(2):
                sa = att or strip(src_att(c), kt_att, 512)
                sg = strip(src_gate(c), 8, 512)
                for m in range(4):
                    for n0, N in HALVES:
                        mo = c * 4 + m
                        b, free = banks.take()
                        tok = accumulate(PS[b][:, :], [(sg[1][:, k, m * 128:(m + 1) * 128], hrhs(k, n0, N))
                                                       for k in range(8)], (free, sg[2], t_hx[0]))
                        tt, ft = tmp.take()
                        ka = act(lambda e, b=b, tt=tt, mo=mo: e.activation(
                            tt, PS[b][:, :], ACT.Tanh, scale=0.5, bias=bcol(mo) if bcol else 0.0), tok, ft, tok_prev)
                        banks.give(b, ka)
                        b, free = banks.take()
                        mc = (c * 4 + m if att else m)
                        tok = accumulate(PS[b][:, :], [(sa[1][:, k, mc * 128:mc * 128 + 128], rhs_att(k, n0, N))
                                                       for k in range(kt_att)], (free, sa[2], tok_r))
                        dst = MX[:, mo, n0:n0 + 512]
                        if first:
                            k = dve(lambda e, b=b, tt=tt, dst=dst: e.scalar_tensor_tensor(
                                out=dst, in0=tt, scalar=1.0, in1=PS[b][:, :], op0=ALU.add, op1=ALU.mult), tok, ka,
                                tok_prev)
                            banks.give(b, k)
                        else:
                            k = dve(lambda e, b=b, tt=tt: e.scalar_tensor_tensor(
                                out=tt, in0=tt, scalar=1.0, in1=PS[b][:, :], op0=ALU.add, op1=ALU.mult), tok, ka)
                            banks.give(b, k)
                            k = gp(lambda e, tt=tt, dst=dst: e.tensor_tensor(dst, dst, tt, ALU.add), k)
                        tmp.give(tt, k)
                        if between:
                            between()
                if not att:
                    done(sa, tok)
                done(sg, tok)
            return k

        t_hx = [t_h]
        MX = R3(F2, 8, 1024)
        phase = everyone()
        mods = ctx.enter_context(nc.sbuf_tensor("mods", [P, 64], F32))
        sc2 = ctx.enter_context(nc.sbuf_tensor("sc2", [P, 16], F32))
        k = act(lambda e: e.activation(sc2[:, :], V("c2", 0, 16), ACT.Tanh, scale=0.5), t_vec)
        k = dve(lambda e: e.scalar_tensor_tensor(out=sc2[:, :], in0=sc2[:, :], scalar=1.0, in1=V("c2", 0, 16),
                                                 op0=ALU.add, op1=ALU.mult), k)
        t_sc = dve(lambda e: e.tensor_scalar(sc2[:, :], sc2[:, :], 0.5, None, ALU.mult), k)
        sc3 = sc2[:, :].rearrange("p (k b) -> p k b", b=2)

        def ada(s, raw, tok, acc):
            nb = 2 if s < 8 else 1
            for i in range(nb):
                a = acc[i]
                k = dve(lambda e: e.tensor_scalar(a, raw[:, 0, :], sc3[:, 0, i:i + 1], None, ALU.mult), tok, t_sc,
                        ada_pe[0])
                for kk in range(1, 8):
                    k = dve(lambda e: e.scalar_tensor_tensor(out=a, in0=raw[:, kk, :], scalar=sc3[:, kk, i:i + 1],
                                                             in1=a, op0=ALU.mult, op1=ALU.add), k)
            return k

        def ada_sum(s, acc):
            nb = 2 if s < 8 else 1
            k = dve.last()
            b, free = banks.take()
            for i in range(nb):
                for m in range(2):
                    t = accumulate(PS[b][:, i * 2 + m:i * 2 + m + 1], [(acc[i][:, m * 128:(m + 1) * 128], onec)],
                                   (free, k, t_onec))
            ada_pe[0] = t
            for i in range(nb):
                k = dve(lambda e: e.tensor_tensor(mods[:, i * 48 + s * 2:i * 48 + s * 2 + 2], PS[b][:, i * 2:i * 2 + 2],
                                                  V("bada", s * 2, 2), ALU.add), t, t_vec)
            banks.give(b, k)

        ada_pe = [None]
        onec_t = ctx.enter_context(nc.sbuf_tensor("onec", [P, 1], F32))
        onec = onec_t[:, :]
        t_onec = gp(lambda e: e.memset(onec, 1.0))

        adq = [R3(F2 + 8192, 8, 256), [R(CB + 512, 256), R(CB + 768, 256)], stream("ada"), [None], [0]]

        def ada_piece():
            raw, acc, sem, relr, cnt = adq
            n = cnt[0]
            cnt[0] += 1
            if 0 < n <= 24:
                ada_sum(n - 1, acc)
            if n < 24:
                tok = act.dma(raw, d["w_ada"][:, n * 256:(n + 1) * 256].rearrange("(k p) n -> p k n", p=P), sem,
                              relr[0], phase)
                relr[0] = ada(n, raw, tok, acc)

        tmpx = Pool_([R(CB + 1024 + i * 512, 512) for i in range(5)])
        wa = strip(d["w_att_o"], 4, 1024)
        sigmoid_mix(MX, None, 4, lambda k, n0, N: YA[:, k, n0 // 64:(n0 + N) // 64, :],
                    lambda c: w_in[:, 3584 + c * 512:4096 + c * 512], lambda m: hb[:, 64 + m:65 + m], True, t_ya, tmpx,
                    phase, att=wa, between=ada_piece)
        t_free0 = pe.last()
        done(wa, t_free0)
        k = sigmoid_mix(MX, lambda c: d["w_rec_o"][:, c * 512:(c + 1) * 512], 8,
                        lambda k, n0, N: RC[:, k, n0:n0 + N],
                        lambda c: w_in[:, 4608 + c * 512:5120 + c * 512], lambda m: hb[:, 72 + m:73 + m], False,
                        t_rc, tmpx, phase, between=ada_piece)
        dump("mix1", MX, k, dve.last())
        t_mx = [k, dve.last()]
        t_x = sp.dma(X, d["x"].rearrange("(t p) n -> p t n", p=P), stream("ldx2"), t_free0)

        def w_out_pass(src, X, MXv, t_mx, t_x, gate=None, tmp=None):
            for c in range(2):
                st = strip(src[:, c * 512:(c + 1) * 512], 8, 512)

                def ev(t, o, tok, c=c):
                    dst = X[:, t, c * 512:(c + 1) * 512]
                    if gate is None:
                        return dve(lambda e: e.scalar_tensor_tensor(out=dst, in0=o, scalar=0.5, in1=dst, op0=ALU.mult,
                                                                    op1=ALU.add), tok, t_x)
                    tt, ft = tmp.take()
                    k = dve(lambda e: e.scalar_tensor_tensor(out=tt, in0=o, scalar=0.5, in1=gate[0][:, c * 512:c * 512 + 512],
                                                             op0=ALU.mult, op1=ALU.mult), tok, ft, gate[1])
                    k2 = gp(lambda e: e.tensor_tensor(dst, dst, tt, ALU.add), k, t_x)
                    tmp.give(tt, k2)
                    return k
                done(st, dense_tm(st, lambda k, t: MXv[:, k, t * 128:(t + 1) * 128], range(8), 512, ev, t_mx))

        w_out_pass(d["w_out"], X, MX, t_mx, t_x)
        t_x = dve.last()
        dump("x1", X, t_x)

        HH, HL = Q3(0, 8, 1024), Q3(8192, 8, 1024)
        fsem = [stream("f0"), stream("f1")]
        FW, FF_F, FT = 30720, 38912, 51200

        def feed_forward(X, w1, w2, t_h, t_x, phase, gate=None):
            raws = Pool_([0, 1])
            for q in (0, 1):
                raws.free[q] = (q, phase)
            splits = Pool_([FW, FW + 4096])
            fb = Pool_([FF_F, FF_F + 4096, FF_F + 8192])
            tmp = Pool_([TMP[:, 0:512], TMP[:, 512:1024]])
            tmg = Pool_([R(21504, 512), R(22016, 512)])
            frel = {}

            def fetch(src, kt, n):
                q, free = raws.take()
                raw = RAW[:, q * 2048:q * 2048 + kt * n].rearrange("p (a b) -> p a b", a=kt)
                return q, raw, sp.dma(raw, src.rearrange("(k p) n -> p k n", p=P), fsem[q], free)

            def weights(src, kt, n):
                q, raw, tok = fetch(src, kt, n)
                s, fs = splits.take()
                hi, lo = Q3(s, kt, n), Q3(s + 2048, kt, n)
                t = split(raw, hi, lo, tok, fs, phase)
                raws.give(q, t)
                return s, hi, lo, t

            def products(o, trios, toks):
                return accumulate(o, [p for a, b, c, d_ in trios for p in ((b, c), (a, d_), (a, c))], toks)

            held = []

            def up(i, w):
                s, hi, lo, tw = w
                f, ffree = fb.take()
                fh, fl = Q3(f, 2, 1024), Q3(f + 2048, 2, 1024)
                for m in range(2):
                    for n0, N in HALVES:
                        b, free = banks.take()
                        cs = slice(m * 128, m * 128 + 128)
                        tok = products(PS[b][:, :], [(hi[:, k, cs], lo[:, k, cs], HH[:, k, n0:n0 + N],
                                                      HL[:, k, n0:n0 + N]) for k in range(8)], (free, tw, t_h))
                        tt, ft = tmp.take()
                        k = act(lambda e: e.activation(tt, PS[b][:, :], ACT.Relu), tok, ft)
                        banks.give(b, k)
                        k = gp(lambda e: e.tensor_tensor(tt, tt, tt, ALU.mult), k)
                        k = split(tt, fh[:, m, n0:n0 + N], fl[:, m, n0:n0 + N], k, ffree, phase)
                        tmp.give(tt, k)
                splits.give(s, tok)
                held.append((f, fh, fl, k))

            def down(i, w):
                c, n = divmod(i, 2)
                s, hi, lo, tw = w
                two = held[:2]
                for t in range(8):
                    b, free = banks.take()
                    ts = slice(t * 128, t * 128 + 128)
                    tok = accumulate(PS[b][:, :], [p for k in range(4) for p in (
                        (two[k // 2][2][:, k % 2, ts], hi[:, k, :]), (two[k // 2][1][:, k % 2, ts], lo[:, k, :]),
                        (two[k // 2][1][:, k % 2, ts], hi[:, k, :]))], (free, tw, two[0][3], two[1][3]))
                    dst = X[:, t, n * 512:(n + 1) * 512]
                    if gate is None:
                        k = dve(lambda e: e.tensor_tensor(dst, dst, PS[b][:, :], ALU.add), tok, t_x,
                                xt.get((t, n)))
                        banks.give(b, k)
                    else:
                        tt, ft = tmg.take()
                        k = dve(lambda e: e.tensor_tensor(tt, PS[b][:, :], gate[0][:, n * 512:n * 512 + 512],
                                                          ALU.mult), tok, ft, gate[1])
                        banks.give(b, k)
                        k = gp(lambda e: e.tensor_tensor(dst, dst, tt, ALU.add), k, t_x, xt.get((t, n)))
                        tmg.give(tt, k)
                    xt[(t, n)] = k
                splits.give(s, tok)
                if n == 1:
                    for f, _, _, _ in two:
                        fb.give(f, tok)
                    del held[:2]

            xt = {}
            jobs = [("u", 0), ("u", 1)]
            for c in range(8):
                if 2 * c + 2 < 16:
                    jobs.append(("u", 2 * c + 2))
                jobs += [("d", 2 * c), ("d", 2 * c + 1)]
                if 2 * c + 3 < 16:
                    jobs.append(("u", 2 * c + 3))

            def get(job):
                kind, i = job
                if kind == "u":
                    return weights(w1[:, i * 256:(i + 1) * 256], 8, 256)
                c, n = divmod(i, 2)
                return weights(w2[c * 512:(c + 1) * 512, n * 512:(n + 1) * 512], 4, 512)

            w = get(jobs[0])
            for n, job in enumerate(jobs):
                nxt = get(jobs[n + 1]) if n + 1 < len(jobs) else None
                (up if job[0] == "u" else down)(job[1], w)
                w = nxt
            return list(xt.values())

        phase = everyone()
        xn = Pool_([R3(F1, 4, 1024), R3(F1 + 4096, 4, 1024)])
        tk = norm_stats(Xt, 8, rs, R(CB, 1024), [t_x, phase])
        tmn = Pool_([TMP[:, i * 512:i * 512 + 512] for i in range(4)])
        t_h = norm_T3(Xt, rs, xn, lambda k: V("ln2", k), None, (HH, HL), tmn, [tk, phase], phase)
        t_x = feed_forward(X, d["w_ff1"], d["w_ff2"], t_h, t_x, everyone())
        phase = everyone()
        for q in range(3):
            wring.free[q] = (wring.free[q][0], phase)
        t_l = load(R(F2, 1024), d["rows"][:, ROW["lnf"][0]:ROW["lnf"][0] + 1024], phase)
        tk = norm_stats(Xt, 8, rs, R(CB, 1024), [t_x, phase])
        for t in range(8):
            t_x = dve(lambda e, t=t: e.scalar_tensor_tensor(out=X[:, t, :], in0=X[:, t, :], scalar=rs[:, t:t + 1],
                                                            in1=R(F2, 1024), op0=ALU.mult, op1=ALU.mult), tk, t_l)
        dump("xf", X, t_x)
        if upto < 2:
            return finish(nc, ctx, (pe, dve, act, gp, sp), out, X, t_x, dbg)

        phase = everyone()
        t_stash = sp.dma(xs.rearrange("(t p) n -> p t n", p=P), X, stream("stash"), t_x)
        gs = ctx.enter_context(nc.sbuf_tensor("gs", [P, 24], F32))
        t_gs = dve(lambda e: e.scalar_tensor_tensor(out=gs[:, 0:8], in0=mods[:, 8:16], scalar=1.0, in1=V("g1", 0, 8),
                                                    op0=ALU.add, op1=ALU.mult), dve.last())
        t_gs = dve(lambda e: e.scalar_tensor_tensor(out=gs[:, 8:16], in0=mods[:, 56:64], scalar=1.0, in1=V("g1", 0, 8),
                                                    op0=ALU.add, op1=ALU.mult))
        t_gs = dve(lambda e: e.scalar_tensor_tensor(out=gs[:, 16:24], in0=mods[:, 32:40], scalar=1.0,
                                                    in1=V("g2", 0, 8), op0=ALU.add, op1=ALU.mult))
        Cx = R3(F2, 2, 1024)
        t_c = load(Cx, d["ctx_2"].rearrange("(t p) n -> p t n", p=P), phase, t_x)
        xn = Pool_([R3(F1, 4, 1024), R3(F1 + 4096, 4, 1024)])
        rc = sm[:, 32:34]
        tk = norm_stats(Xt, 8, rs, R(CB, 1024), [t_x, phase])
        tk2 = norm_stats(lambda t: Cx[:, t, :], 2, rc, R(CB, 1024), [t_c, phase])
        ta = norm_T(Xt, 8, rs, xn, lambda k: gs[:, k:k + 1], lambda k: mods[:, k:k + 1], 0, [tk, phase, t_gs], [phase, t_gs])
        tb = norm_T(lambda t: Cx[:, t, :], 2, rc, xn, lambda k: gs[:, 8 + k:9 + k],
                    lambda k: mods[:, 48 + k:49 + k], 1024, [tk2, phase, t_gs], phase)
        t_h = [ta, tb]
        t_hx[0] = t_h
        dump("h2", HT[:, :, :], t_h)
        w2 = d["w_in_2"]

        phase = [everyone(), t_stash]
        kT = R3(F0, 4, 1280)
        qT = R3(F0 + 5120, 4, 1024)
        kt = R3(F0 + 9216, 10, 512)
        vt = R3(F0 + 14336, 10, 512)
        O = R3(F0 + 19456, 8, 512)
        XT = F0 + 23552
        lv = A[:, CB:CB + 1792].rearrange("p (d l f) -> p d l f", d=2, l=LEVELS)
        cum = R3(CB + 1792, 2, 128)
        neg = R3(CB + 2048, 2, 128)
        ones = R(CB + 2304, 128)
        AB = R3(CB + 2432, 10, 32)
        stb = R3(CB + 2752, 2, 32)
        rw = R(CB + 2816, 32)
        gneg = R3(CB + 2848, 10, 16)
        t_lv = load(lv, d["lv"], phase)
        t_cum = load(cum, d["cum"], phase)
        t_neg = load(neg, d["neg"], phase)
        t_rw = load(rw, d["rows"][:, ROW["dt"][0]:ROW["dt"][0] + 32], phase)
        t_one = gp(lambda e: e.memset(ones, 1.0), phase)
        st = strip(w2[:, 2816:2848], 8, 32)
        done(st, dense_tm(st, hlhs, range(10), 32,
                          lambda t, o, tok: act(lambda e: e.activation(AB[:, t, :], o, ACT.Copy), tok, phase), t_h))
        k = act.last()
        ka = act(lambda e: e.activation(rw[:, 16:32], rw[:, 16:32], ACT.Exp), t_rw)
        ga3 = AB[:, :, 0:16]
        be3 = AB[:, :, 16:32]
        tg1 = R3(XT, 10, 16)
        tg2 = R3(XT + 160, 10, 16)
        k1 = dve(lambda e: e.tensor_tensor(ga3, ga3, bc(rw[:, 0:16].unsqueeze(1), [P, 10, 16]), ALU.add), k, t_rw)
        k2 = act(lambda e: e.activation(tg1, ga3, ACT.Abs), k1)
        k2 = act(lambda e: e.activation(tg1, tg1, ACT.Exp, scale=-1.0), k2)
        k2 = act(lambda e: e.activation(tg1, tg1, ACT.Ln, bias=1.0), k2)
        k3 = dve(lambda e: e.tensor_scalar(tg2, ga3, 0.0, None, ALU.max), k1)
        k3 = dve(lambda e: e.tensor_tensor(tg2, tg2, tg1, ALU.add), k2, k3)
        k3 = dve(lambda e: e.tensor_tensor(gneg, tg2, bc(rw[:, 16:32].unsqueeze(1), [P, 10, 16]), ALU.mult), k3, ka)
        k3 = dve(lambda e: e.tensor_scalar(ga3, gneg, -1.0, None, ALU.mult), k3)
        k4 = act(lambda e: e.activation(be3, be3, ACT.Tanh, scale=0.5), k2)
        t_ab = dve(lambda e: e.tensor_scalar(be3, be3, 0.5, 0.5, ALU.mult, ALU.add), k4, k3)
        dump("ab", AB, t_ab)

        PIECES = [(0, 512), (512, 512), (1024, 256)]
        t0 = F0 + 19456
        raws2 = [R(t0, 1288), R(t0 + 1288, 1288)]
        xc = R(t0 + 2576, 1280)
        th_ = R(t0 + 3856, 1280)
        sq = R3(t0 + 3856, 10, 128)
        qt = R3(t0 + 5136, 10, 128)
        nr = R(CB + 3664, 20)
        for r_ in raws2:
            tz = gp(lambda e: e.memset(r_, 0.0), phase)
        crel = {}
        tiles = [(which, col, m) for which, col in ((1, 1280), (0, 768), (2, 1792)) for m in range(4)]

        def conv_in(i):
            which, col, m = tiles[i]
            raw = raws2[i % 2]
            if m == 0:
                crel["st"] = strip(w2[:, col:col + 512], 8, 512)
            tok = dense_fm(crel["st"], hrhs, PIECES if which else HALVES,
                           lambda mm, n0, N, o, tk: act(lambda e: e.activation(
                               raw[:, (1 + n0 if n0 < 1024 else 3 + n0):(1 + n0 if n0 < 1024 else 3 + n0) + N], o,
                               ACT.Copy), tk, tz, crel.get(("raw", i % 2))), t_h, mts=[m])
            crel[("in", i)] = act.last()
            if m == 3:
                done(crel["st"], tok)

        def conv_norm(i):
            which, col, m = tiles[i]
            raw = raws2[i % 2]
            tr = crel.pop(("in", i))
            NT = 10 if which else 8
            segs = ((1, 0, 1024), (1027, 1024, 256)) if which else ((1, 0, 1024),)
            n = NT * 128
            cwi = lambda j: V("cw2", j * 12 + which * 4 + m)
            for so, do, sn in segs:
                k = dve(lambda e: e.tensor_scalar(xc[:, do:do + sn], raw[:, so - 1:so - 1 + sn], cwi(0), None,
                                                  ALU.mult), tr, crel.get("xc"))
                for j in (1, 2):
                    k = dve(lambda e: e.scalar_tensor_tensor(
                        out=xc[:, do:do + sn], in0=raw[:, so - 1 + j:so - 1 + j + sn], scalar=cwi(j),
                        in1=xc[:, do:do + sn], op0=ALU.mult, op1=ALU.add), k)
            crel[("raw", i % 2)] = k
            k2 = act(lambda e: e.activation(th_[:, 0:n], xc[:, 0:n], ACT.Tanh, scale=0.5), k, crel.get("sq"))
            k = dve(lambda e: e.scalar_tensor_tensor(out=xc[:, 0:n], in0=th_[:, 0:n], scalar=1.0,
                                                     in1=xc[:, 0:n], op0=ALU.add, op1=ALU.mult), k2)
            crel["sq"] = k
            got = []
            for h in range(0, NT, 4):
                n4 = min(4, NT - h)
                b, free = banks.take()
                for t in range(n4):
                    tp = pe(lambda e: e.transpose(
                        PS[b][:, t * 128:(t + 1) * 128], xc[:, (h + t) * 128:(h + t + 1) * 128], ident[:, :]), free, k)
                got.append((h, n4, b))
            crel["xc"] = tp
            if which == 2:
                for h, n4, b in got:
                    k = act(lambda e: e.activation(
                        vt[:, h:h + n4, m * 128:(m + 1) * 128],
                        PS[b][:, 0:n4 * 128].rearrange("p (t f) -> p t f", f=128), ACT.Copy, scale=0.5), tp, phase)
                    banks.give(b, k)
                return
            for h, n4, b in got:
                k = act(lambda e: e.activation(
                    sq[:, h:h + n4, :], PS[b][:, 0:n4 * 128].rearrange("p (t f) -> p t f", f=128), ACT.Square), tp)
            n2 = NT * 2
            k = dve(lambda e: e.tensor_reduce(
                nr[:, 0:n2], sq[:, 0:NT, :].rearrange("p t (s f) -> p (t s) f", f=64), AX.X, ALU.add), k)
            crel["sq"] = k
            fac = 1.0 if which else 64.0
            k = dve(lambda e: e.tensor_scalar(nr[:, 0:n2], nr[:, 0:n2], fac, 4 * EPS * fac, ALU.mult, ALU.add), k)
            k = act(lambda e: e.activation(nr[:, 0:n2], nr[:, 0:n2], ACT.Sqrt), k)
            k = dve(lambda e: e.reciprocal(nr[:, 0:n2], nr[:, 0:n2]), k)
            for h, n4, b in got:
                dst = (kt[:, h:h + n4, m * 128:(m + 1) * 128] if which else qt[:, h:h + n4, :])
                for s in range(2):
                    kk = dve(lambda e: e.tensor_tensor(
                        dst[:, :, s * 64:s * 64 + 64],
                        PS[b][:, 0:n4 * 128].rearrange("p (t s f) -> p t s f", s=2, f=64)[:, :, s, :],
                        bc(nr[:, h * 2 + s:(h + n4) * 2:2].unsqueeze(2), [P, n4, 64]), ALU.mult), k,
                        phase, crel.get("qt") if not which else None)
                banks.give(b, kk)
            crel[("tok", i)] = kk

        def conv_back(i):
            which, col, m = tiles[i]
            if which == 2:
                return
            kk = crel.pop(("tok", i))
            NT = 10 if which else 8
            for h in range(0, NT, 4):
                n4 = min(4, NT - h)
                b, free = banks.take()
                for t in range(n4):
                    src = kt[:, h + t, m * 128:(m + 1) * 128] if which else qt[:, h + t, :]
                    tp = pe(lambda e: e.transpose(PS[b][:, t * 128:(t + 1) * 128], src, ident[:, :]), free, kk)
                dstT = (kT if which else qT)[:, m, h * 128:(h + n4) * 128]
                k = act(lambda e: e.activation(dstT, PS[b][:, 0:n4 * 128], ACT.Copy), tp, phase)
                banks.give(b, k)
            if not which:
                crel["qt"] = tp

        pipeline(12, [conv_in, conv_back, conv_norm], [0, 2, 1])
        t_kv = [act.last(), dve.last(), pe.last()]
        dump("kT", kT, t_kv)
        dump("qT", qT, t_kv)
        dump("vt", vt, t_kv)

        phase = everyone()
        slots = [wring.take() for _ in range(3)]
        wfree = [f for _, f in slots]
        t_sp = sp.dma(hs, R(HT0, 10240), stream("spill"), phase)
        wfree.append(t_sp)
        M4 = lambda off: A[:, off:off + 1024].rearrange("p (h f) -> p h f", h=8)
        AT = [[M4(i * 1024) for i in range(2)], [M4(HT0 + i * 1024) for i in range(2)]]
        IT = [[M4(2048 + i * 1024) for i in range(2)], [M4(HT0 + 2048 + i * 1024) for i in range(2)]]
        Y = [M4(4096 + i * 1024) for i in range(2)]
        YTS = [[M4(6144 + i * 1024) for i in range(2)], [M4(HT0 + 4096 + i * 1024) for i in range(2)]]
        GG = M4(HT0 + 6144)
        grel = [None]
        IM = [M4(8192 + i * 1024) for i in range(2)]
        LK = [M4(10240 + i * 1024) for i in range(2)]
        SB = [R3(XT + i * 512, 4, 128) for i in range(2)]
        ub_ = [R3(XT + 1024 + i * 512, 8, 64) for i in range(2)]
        rb_ = [R3(CB + 3072, 8, 64), R3(XT + 2048, 8, 64)]
        sml = A[:, HT0 + 7168:HT0 + 7328].rearrange("p (a b c) -> p a b c", a=2, b=2)
        for dd in range(2):
            gp(lambda e, dd=dd: e.memset(SB[dd], 0.0), phase)
        t_S = [gp.last(), gp.last()]
        o_tok = [None] * 8
        rel = [{}, {}]
        rows2 = lambda s: slice(64 * s, 64 * s + 64)

        def hv(b):
            return PS[b][:, :].rearrange("p (a f) -> p a f", a=4)

        def each_head(mk, toks, n=128):
            res = []
            for s in range(2):
                b, free = banks.take()
                for j in range(4):
                    l, r = mk(s, j)
                    tok = accumulate(PS[b][:, j * n:(j + 1) * n], [(l, r)], (free, toks))
                res.append((b, tok))
            return res

        def delta_prep(dd, t, par):
            r = rel[dd]
            g = AB[:, t, dd * 8:dd * 8 + 8]
            be = AB[:, t, 16 + dd * 8:24 + dd * 8]
            sv = sml[:, par, dd, :]
            b, free = banks.take()
            tok = accumulate(PS[b][:, 0:8], [(cum[:, dd, :], g)], (free, t_ab, t_cum))
            tok = accumulate(PS[b][:, 8:16], [(ones, g)], (t_one,))
            k1 = dve(lambda e, b=b: e.tensor_scalar(sv[:, 0:8], PS[b][:, 0:8], -1.0, None, ALU.mult), tok, r.get(("sv", par)), wfree)
            k1 = dve(lambda e, b=b: e.tensor_copy(sv[:, 8:16], PS[b][:, 8:16]), tok)
            k2 = dve(lambda e: e.tensor_tensor(sv[:, 24:32], sv[:, 8:16], sv[:, 0:8], ALU.add), k1)
            banks.give(b, k1)
            k3 = act(lambda e: e.activation(sv[:, 16:24], sv[:, 0:8], ACT.Exp, scale=-1.0), k1)
            k3 = act(lambda e: e.activation(sv[:, 24:32], sv[:, 24:32], ACT.Exp), k2)
            k3 = act(lambda e: e.activation(sv[:, 32:40], sv[:, 8:16], ACT.Exp), k1)
            r[("svt", par)] = k3
            G8 = GG
            kq = dve(lambda e: e.tensor_tensor(G8, bc(g.unsqueeze(2), [P, 8, 128]),
                                               bc(cum[:, dd, :].unsqueeze(1), [P, 8, 128]), ALU.mult),
                     t_ab, t_cum, wfree, grel[0])
            E = IT[par][dd]
            for s in range(2):
                b, free = banks.take()
                gv = G8.rearrange("p (j s) f -> p s j f", s=2)[:, s, :, :]
                tok = accumulate(PS[b][:, :], [(ones, gv), (ident[:, :], bc(neg[:, dd, :].unsqueeze(1), [P, 4, 128]))],
                                 (free, kq, t_neg, t_one))
                grel[0] = tok
                for j in range(4):
                    ke = act(lambda e, b=b, s=s, j=j: e.activation(
                        E[:, s * 4 + j, :], hv(b)[:, j, :], ACT.Exp, bias=sv[:, 2 * j + s:2 * j + s + 1]), tok, k1,
                        r.get(("it", par)), wfree)
                banks.give(b, ke)
            ti = t * 128
            kk = each_head(lambda s, j: (kT[rows2(s), j, ti:ti + 128], kT[rows2(s), j, ti:ti + 128]), t_kv)
            for s, (b, tok) in enumerate(kk):
                bev = be.rearrange("p (j s) -> p s j", s=2)[:, s, :]
                k = dve(lambda e, b=b, s=s, bev=bev: e.tensor_tensor(
                    AT[par][dd][:, s * 4:s * 4 + 4, :], hv(b), bc(bev.unsqueeze(2), [P, 4, 128]), ALU.mult), tok,
                    r.get(("at", par)), wfree)
                banks.give(b, k)
            ka = gp(lambda e: e.tensor_tensor(AT[par][dd], AT[par][dd], E, ALU.mult), k, ke)
            if t < 8:
                kq = each_head(lambda s, j: (kT[rows2(s), j, ti:ti + 128], qT[rows2(s), j, ti:ti + 128]), t_kv)
                for s, (b, tok) in enumerate(kq):
                    k = dve(lambda e, b=b, s=s: e.tensor_tensor(
                        E[:, s * 4:s * 4 + 4, :], hv(b), E[:, s * 4:s * 4 + 4, :], ALU.mult), tok, ka)
                    banks.give(b, k)
            r[("itt", par)] = k
            r[("att", par)] = ka

        def delta_start(dd, par):
            r = rel[dd]
            ka = r["at_t"] = r[("att", par)]
            YT = YTS[par]
            k = dve(lambda e: e.tensor_tensor(LK[dd], AT[par][dd], bc(lv[:, dd, 0, :].unsqueeze(1), [P, 8, 128]), ALU.mult),
                    ka, t_lv, r.get("lk"), wfree)
            k = dve(lambda e: e.scalar_tensor_tensor(
                out=YT[dd], in0=LK[dd], scalar=-1.0, in1=bc(ident[:, :].unsqueeze(1), [P, 8, 128]), op0=ALU.mult,
                op1=ALU.add), k, r.get(("yt", par)), wfree)
            r["yt_t"] = [k]
            ks = []
            for s in range(2):
                b, free = banks.take()
                for j in range(4):
                    tok = pe(lambda e, b=b, s=s, j=j: e.transpose(hv(b)[:, j, :], YT[dd][:, s * 4 + j, :], ident[:, :]),
                             free, k)
                kk = act(lambda e, b=b, s=s: e.activation(Y[dd][:, s * 4:s * 4 + 4, :], hv(b), ACT.Copy), tok,
                         r.get("y"), wfree)
                banks.give(b, kk)
                ks.append(kk)
            r["y_t"] = ks
            r["lk"] = k

        def level_mask(dd, lev, par):
            r = rel[dd]
            k = gp(lambda e: e.tensor_tensor(LK[dd], AT[par][dd], bc(lv[:, dd, lev, :].unsqueeze(1), [P, 8, 128]),
                                             ALU.mult), r["at_t"], r["lk"])
            r["lk_t"] = k
            r[("at", par)] = k

        def level_a(dd, lev):
            r = rel[dd]
            res = each_head(lambda s, j: (LK[dd][:, s * 4 + j, :], Y[dd][:, s * 4 + j, :]), [r["lk_t"], r["y_t"]])
            r["lk"] = res[-1][1]
            r["im_t"] = []
            for s, (b, tok) in enumerate(res):
                k = dve(lambda e, b=b, s=s: e.scalar_tensor_tensor(
                    out=IM[dd][:, s * 4:s * 4 + 4, :], in0=hv(b), scalar=-1.0,
                    in1=bc(ident[:, :].unsqueeze(1), [P, 4, 128]), op0=ALU.mult, op1=ALU.add), tok, r.get("im"))
                banks.give(b, k)
                r["im_t"].append(k)

        def level_b(dd, lev, par):
            r = rel[dd]
            YT = YTS[par]
            if lev < LEVELS - 1:
                ry = each_head(lambda s, j: (YT[dd][:, s * 4 + j, :], IM[dd][:, s * 4 + j, :]), [r["im_t"], r["yt_t"]])
            rt = each_head(lambda s, j: (IM[dd][:, s * 4 + j, :], YT[dd][:, s * 4 + j, :]), [r["im_t"], r["yt_t"]])
            last = rt[-1][1]
            r["im"] = last
            if lev < LEVELS - 1:
                r["y_t"] = []
                for s, (b, tok) in enumerate(ry):
                    k = act(lambda e, b=b, s=s: e.activation(Y[dd][:, s * 4:s * 4 + 4, :], hv(b), ACT.Copy), tok)
                    banks.give(b, k)
                    r["y_t"].append(k)
            else:
                r["y"] = r["lk"]
            r["yt_t"] = []
            for s, (b, tok) in enumerate(rt):
                k = act(lambda e, b=b, s=s: e.activation(YT[dd][:, s * 4:s * 4 + 4, :], hv(b), ACT.Copy), tok, last)
                banks.give(b, k)
                r["yt_t"].append(k)

        def bcast64(v, shape=(P, 8, 64)):
            return bc(v.unsqueeze(2), list(shape))

        p3 = lambda b: PS[b][:, :].rearrange("p (h f) -> p h f", h=8)
        p4 = lambda b, s: PS[b][rows2(s), :].rearrange("p (j s f) -> p j s f", j=4, s=2)[:, :, s, :]

        def step_a(dd, t, par):
            r = rel[dd]
            sv = sml[:, par, dd, :]
            ti = t * 128
            Rr = rb_[dd]
            b, free = banks.take()
            for j in range(4):
                tok = accumulate(PS[b][:, j * 128:(j + 1) * 128], [(kT[:, j, ti:ti + 128], SB[dd][:, j, :])],
                                 (free, t_S[dd], t_kv))
            k = dve(lambda e: e.tensor_tensor(Rr, p3(b), bcast64(sv[:, 16:24]), ALU.mult), tok, r[("svt", par)],
                    r.get("r"))
            banks.give(b, k)
            r["rt"] = dve(lambda e: e.tensor_tensor(Rr, vt[:, t, :].rearrange("p (h f) -> p h f", h=8), Rr,
                                                    ALU.subtract), k)

        def step_b(dd, t, par):
            r = rel[dd]
            sv = sml[:, par, dd, :]
            be = AB[:, t, 16 + dd * 8:24 + dd * 8]
            U, Rr = ub_[dd], rb_[dd]
            YT = YTS[par]
            b, free = banks.take()
            for h in range(8):
                i = (h % 2) * 4 + h // 2
                tok = accumulate(PS[b][:, h * 64:(h + 1) * 64], [(YT[dd][:, i, :], Rr[:, h, :])],
                                 (free, r["rt"], r[("ytt", par)]))
            r[("yt", par)] = tok
            ku = dve(lambda e: e.tensor_tensor(U, p3(b), bcast64(be), ALU.mult), tok, r.get("u"))
            banks.give(b, ku)
            r["ut"] = ku
            r["rt"] = dve(lambda e: e.tensor_tensor(Rr, U, bcast64(sv[:, 24:32]), ALU.mult), ku, tok)

        def step_c(dd, t, par):
            r = rel[dd]
            sv = sml[:, par, dd, :]
            ti = t * 128
            St = SB[dd]
            U, Rr = ub_[dd], rb_[dd]
            ku, kr = r["ut"], r["rt"]
            if t < 8:
                b1, free = banks.take()
                for j in range(4):
                    tq = accumulate(PS[b1][:, j * 128:(j + 1) * 128], [(qT[:, j, ti:ti + 128], St[:, j, :])],
                                    (free, t_kv, t_S[dd]))
                b2, free = banks.take()
                for h in range(8):
                    i = (h % 2) * 4 + h // 2
                    to = accumulate(PS[b2][:, h * 64:(h + 1) * 64], [(IT[par][dd][:, i, :], U[:, h, :])],
                                    (free, ku, r[("itt", par)]))
                r[("it", par)] = r["u"] = to
            else:
                r["u"] = kr
                r[("it", par)] = r[("att", par)]
            b, free = banks.take()
            for j in range(4):
                tok = accumulate(PS[b][:, j * 128:(j + 1) * 128],
                                 [(kt[:, t, j * 128:(j + 1) * 128], Rr[:, 2 * j:2 * j + 2, :])], (free, kr))
            r["r"] = tok
            for s in range(2):
                gl = sv[rows2(s), 32:40].rearrange("p (j s) -> p s j", s=2)[:, s, :]
                Sv = St[rows2(s), :, s * 64:s * 64 + 64]
                k = dve(lambda e: e.tensor_tensor(Sv, Sv, bcast64(gl, (64, 4, 64)), ALU.mult), tok, r[("svt", par)])
                k = dve(lambda e: e.tensor_tensor(Sv, Sv, p4(b, s), ALU.add), k)
            banks.give(b, k)
            t_S[dd] = k
            if t < 8:
                Ot = O[:, t, :].rearrange("p (h f) -> p h f", h=8)
                k = dve(lambda e: e.tensor_tensor(Rr, p3(b1), bcast64(sv[:, 16:24]), ALU.mult), tq, r["r"])
                banks.give(b1, k)
                k2 = dve(lambda e: e.tensor_tensor(Rr, Rr, p3(b2), ALU.add), k, to)
                banks.give(b2, k2)
                if o_tok[t] is None:
                    k3 = gp(lambda e: e.tensor_copy(Ot, Rr), k2, phase)
                else:
                    k3 = gp(lambda e: e.tensor_tensor(Ot, Ot, Rr, ALU.add), k2, o_tok[t])
                o_tok[t] = k3
                r["r"] = k3
            r[("sv", par)] = [dve.last(), r[("svt", par)]]

        orders = [[8, 9] + list(range(8)), [9, 8] + list(range(7, -1, -1))]
        for dd in range(2):
            delta_prep(dd, orders[dd][0], 0)
        for step in range(11):
            par = step % 2
            if step < 10:
                for dd in range(2):
                    delta_start(dd, par)
            for lev in range(1, LEVELS):
                if lev <= 3 and step >= 1:
                    for dd in range(2):
                        (step_a, step_b, step_c)[lev - 1](dd, orders[dd][step - 1], 1 - par)
                if step == 10:
                    continue
                for dd in range(2):
                    level_mask(dd, lev, par)
                for dd in range(2):
                    level_a(dd, lev)
                if lev >= 4 and lev < 6 and step < 9:
                    delta_prep(lev - 4, orders[lev - 4][step + 1], 1 - par)
                for dd in range(2):
                    level_b(dd, lev, par)
            if step < 10:
                for dd in range(2):
                    rel[dd][("ytt", par)] = rel[dd]["yt_t"]
        t_o = gp.last()
        dump("o", O, t_o)
        t_d = everyone()
        for s, _ in slots:
            wring.give(s, t_d)
        t_h = t_hx[0] = [sp.dma(R(HT0, 10240), hs, stream("unspill"), t_d, t_sp)]

        phase = everyone()
        aq = R3(F0, 4, 1024)
        ak = R(F0 + 4096, 1280)
        av = R3(F0 + 5376, 10, 128)
        rope = R3(F0 + 6656, 8, 128)
        gqk = R(F0 + 7680, 640)
        wn = R(F0 + 8320, 384)
        sk = R(F0 + 8704, 8)
        t_rope = load(rope, d["rope"], phase)
        t_gqk = load(gqk, d["rows"][:, ROW["qk"][0]:ROW["qk"][0] + 640], phase)
        t_wn = load(wn, d["wn"], phase)
        t_sk = load(sk, d["rows"][:, ROW["sink"][0]:ROW["sink"][0] + 8], phase)
        T1 = F0 + 8720
        zb = [R(T1 + i * 640, 640) for i in range(3)]
        z2 = [R(T1 + 1920 + i * 640, 640) for i in range(3)]
        z3 = [R(T1 + 3840 + i * 640, 640) for i in range(3)]
        zs = [R(T1 + 5760 + i * 16, 16) for i in range(3)]
        s1 = strip(w2[:, 0:512], 8, 512)
        s2 = strip(w2[:, 512:768], 8, 256)
        zr = [{}, {}, {}]

        def qkv_in(t):
            r = zr[t % 3]
            z = zb[t % 3]
            r["in"] = []
            if t < 8:
                dense_tm(s1, hlhs, [t], 512, lambda t_, o, tok: act(
                    lambda e: e.activation(z[:, 0:512], o, ACT.Copy), tok, r.get("z"), phase), t_h)

            def ev(t_, o, tok):
                act(lambda e: e.activation(z[:, 512:640], o[:, 0:128], ACT.Copy), tok, r.get("z"), phase)
                return act(lambda e: e.activation(av[:, t, :], o[:, 128:256], ACT.Copy), tok, phase)
            dense_tm(s2, hlhs, [t], 256, ev, t_h)
            r["in"] = act.last()

        def qkv_norm(t):
            r = zr[t % 3]
            z, q2, q3, ss = zb[t % 3], z2[t % 3], z3[t % 3], zs[t % 3]
            c0 = 0 if t < 8 else 512
            nh = 10 if t < 8 else 2
            zz, a2, a3, gg = z[:, c0:640], q2[:, c0:640], q3[:, c0:640], gqk[:, c0:640]
            v3 = lambda a: a.rearrange("p (h f) -> p h f", f=64)
            k = dve(lambda e: e.tensor_tensor(a2, zz, zz, ALU.mult), r["in"], r.get("z2"), phase)
            k = dve(lambda e: e.tensor_reduce(ss[:, 0:nh], v3(a2), AX.X, ALU.add), k, r.get("ss"), phase)
            k = dve(lambda e: e.tensor_scalar(ss[:, 0:nh], ss[:, 0:nh], 1.0 / 64, EPS, ALU.mult, ALU.add), k)
            k = act(lambda e: e.activation(ss[:, 0:nh], ss[:, 0:nh], ACT.Sqrt), k)
            k = dve(lambda e: e.reciprocal(ss[:, 0:nh], ss[:, 0:nh]), k)
            k = dve(lambda e: e.tensor_tensor(v3(zz), v3(zz), bc(ss[:, 0:nh].unsqueeze(2), [P, nh, 64]), ALU.mult), k)
            r["ss"] = k
            k = dve(lambda e: e.tensor_tensor(zz, zz, gg, ALU.mult), k, t_gqk)
            if t < 8:
                cs, sn = rope[:, t, 0:64], rope[:, t, 64:128]
                ka = dve(lambda e: e.tensor_tensor(v3(a2), v3(zz), bc(cs.unsqueeze(1), [P, nh, 64]), ALU.mult), k,
                         t_rope)
                v5 = lambda a: a.rearrange("p (h g s f) -> p h g s f", g=2, s=2, f=16)
                sn5 = sn.rearrange("p (g s f) -> p g s f", g=2, s=2)
                for g in range(2):
                    for s in range(2):
                        kb = dve(lambda e, g=g, s=s: e.tensor_tensor(
                            v5(a3)[:, :, g, s, :], v5(zz)[:, :, g, 1 - s, :],
                            bc(sn5[:, g, s, :].unsqueeze(1), [P, 10, 16]), ALU.mult), k, r.get("z3"), t_rope, phase)
                k = dve(lambda e: e.tensor_tensor(zz, a2, a3, ALU.add), ka, kb)
            r["z2"] = r["z3"] = k
            r["n"] = k
            if t < 8:
                qp = q2[:, 0:512].rearrange("p (j s f) -> p j s f", j=4, s=2)
                for s in range(2):
                    kp = gp(lambda e, s=s: e.tensor_copy(
                        qp[:, :, s, :], z[:, s * 256:(s + 1) * 256].rearrange("p (j f) -> p j f", f=64)), k)
                r["np"] = kp

        def qkv_T(t):
            r = zr[t % 3]
            z, q2 = zb[t % 3], z2[t % 3]
            k = r["n"]
            b, free = banks.take()
            if t < 8:
                kp = r["np"]
                for j in range(4):
                    tp = pe(lambda e, j=j: e.transpose(PS[b][:, j * 128:(j + 1) * 128],
                                                       q2[:, j * 128:(j + 1) * 128], ident[:, :]), free, kp)
                ke = act(lambda e: e.activation(aq[:, :, t * 128:(t + 1) * 128], hv(b), ACT.Copy), tp, phase)
                banks.give(b, ke)
                b, free = banks.take()
                r["z2"] = tp
            tp = pe(lambda e: e.transpose(PS[b][:, 0:128], z[:, 512:640], ident[:, :]), free, k)
            ke = act(lambda e: e.activation(ak[:, t * 128:(t + 1) * 128], PS[b][:, 0:128], ACT.Copy), tp, phase)
            banks.give(b, ke)
            r["z"] = tp

        pipeline(10, [qkv_in, qkv_norm, qkv_T], [0, 1, 2])
        done(s1, pe.last())
        done(s2, pe.last())
        t_q = [act.last()]
        dump("aq", aq, t_q)
        dump("ak", ak, t_q)

        sc_ = Pool_([R(T1 + i * 640, 640) for i in range(3)])
        pp_ = Pool_([R(T1 + 1920 + i * 640, 640) for i in range(5)])
        pT_ = Pool_([R3(T1 + 5120 + i * 640, 5, 128) for i in range(4)])
        phase = everyone()
        su = {}
        wst = ctx.enter_context(nc.sbuf_tensor("wst", [P, 8, 4], F32))

        def unit(i):
            n, r = divmod(i, 8)
            j, s = divmod(r, 2)
            return n, j, s, j + 4 * s

        def watt_scores(i):
            n, j, s, h = unit(i)
            lo, hi = max(n - 1, 0), min(n + 2, 8)
            nl = (hi - lo) * 128
            m0 = (lo - (n - 1)) * 128
            q = aq[rows2(s), j, n * 128:(n + 1) * 128]
            b1, f1 = banks.take()
            ta = accumulate(PS[b1][:, 0:nl], [(q, ak[rows2(s), lo * 128:hi * 128])], (f1, t_q))
            b2, f2 = banks.take()
            tb = accumulate(PS[b2][:, 0:256], [(q, ak[rows2(s), 1024:1280])], (f2,))
            c = wst[:, i % 8, :]
            z, fz = sc_.take()
            k = dve(lambda e: e.scalar_tensor_tensor(out=z[:, 0:nl], in0=PS[b1][:, 0:nl], scalar=0.125,
                                                     in1=wn[:, m0:m0 + nl], op0=ALU.mult, op1=ALU.add), ta, fz, t_wn,
                    phase)
            banks.give(b1, k)
            kb = dve(lambda e: e.tensor_scalar(z[:, nl:nl + 256], PS[b2][:, 0:256], 0.125, None, ALU.mult), tb, fz)
            banks.give(b2, kb)
            k = dve(lambda e: e.tensor_reduce(c[:, 0:1], z[:, 0:nl + 256], AX.X, ALU.max), kb, k)
            k = dve(lambda e: e.tensor_scalar(c[:, 0:1], c[:, 0:1], sk[:, h:h + 1], -1.0, ALU.max, ALU.mult), k, t_sk)
            p, fp = pp_.take()
            ke = act(lambda e: e.activation(p[:, 0:nl + 256], z[:, 0:nl + 256], ACT.Exp, bias=c[:, 0:1],
                                            accum_out=c[:, 1:2]), k, fp, phase)
            sc_.give(z, ke)
            kf = act(lambda e: e.activation(c[:, 2:3], sk[:, h:h + 1], ACT.Exp, bias=c[:, 0:1]), k)
            su[i] = (p, c, [kf, ke], lo, hi)

        def watt_scale(i):
            p, c, kf, lo, hi = su[i]
            nl = (hi - lo) * 128
            k = dve(lambda e: e.tensor_tensor(c[:, 1:2], c[:, 1:2], c[:, 2:3], ALU.add), kf)
            k = dve(lambda e: e.reciprocal(c[:, 3:4], c[:, 1:2]), k)
            k = gp(lambda e: e.tensor_scalar(p[:, 0:nl + 256], p[:, 0:nl + 256], c[:, 3:4], None, ALU.mult), k)
            su[i] = (p, k, lo, hi)

        def watt_tr(i):
            p, k, lo, hi = su[i]
            nt = hi - lo + 2
            q, fq = pT_.take()
            for c0 in range(0, nt, 4):
                n4 = min(4, nt - c0)
                b, free = banks.take()
                for c in range(n4):
                    tp = pe(lambda e, b=b, c=c, c0=c0: e.transpose(
                        PS[b][:, c * 128:(c + 1) * 128], p[:, (c0 + c) * 128:(c0 + c + 1) * 128], ident[:, :]), free, k)
                ke = act(lambda e, b=b, n4=n4, c0=c0: e.activation(
                    q[:, c0:c0 + n4, :], PS[b][:, 0:n4 * 128].rearrange("p (a f) -> p a f", f=128), ACT.Copy), tp, fq)
                banks.give(b, ke)
            pp_.give(p, tp)
            su[i] = (q, ke, lo, hi)

        def watt_pv(i):
            n, j, s, h = unit(i)
            q, ke, lo, hi = su.pop(i)
            tl = list(range(lo, hi)) + [8, 9]
            if s == 0:
                su["b"] = banks.take()
            b, free = su["b"]
            tok = accumulate(PS[b][64 * s:64 * s + 64, 0:128],
                             [(av[:, t, s * 64:s * 64 + 64], q[:, x, :]) for x, t in enumerate(tl)], (free, ke))
            pT_.give(q, tok)
            if s == 1:
                k = dve(lambda e: e.tensor_copy(aq[:, j, n * 128:(n + 1) * 128], PS[b][:, 0:128]), tok)
                banks.give(b, k)

        pipeline(64, [watt_scores, watt_scale, watt_tr, watt_pv], [0, 1, 3, 4])
        t_ya = dve.last()
        dump("ya2", aq, t_ya)

        phase = everyone()
        yd = R3(T1, 4, 1024)
        zz_ = [R(T1 + 4096 + i * 512, 512) for i in range(2)]
        th2 = [R(T1 + 5120 + i * 512, 512) for i in range(2)]
        dn = R(T1 + 6144, 512)
        t_dn = load(dn, d["rows"][:, ROW["dn"][0]:ROW["dn"][0] + 512], phase)
        ss8 = sm[:, 0:64].rearrange("p (t h) -> p t h", h=8)
        v3 = lambda a: a.rearrange("p (h f) -> p h f", f=64)
        for t in range(8):
            q2 = th2[t % 2]
            k = dve(lambda e, t=t, q2=q2: e.tensor_tensor(q2, O[:, t, :], O[:, t, :], ALU.mult), t_o, phase)
            k = dve(lambda e, t=t, q2=q2: e.tensor_reduce(ss8[:, t, :], v3(q2), AX.X, ALU.add), k)
        k = dve(lambda e: e.tensor_scalar(sm[:, 0:64], sm[:, 0:64], 1.0 / 64, EPS, ALU.mult, ALU.add), k)
        k = act(lambda e: e.activation(sm[:, 0:64], sm[:, 0:64], ACT.Sqrt), k)
        t_ss = dve(lambda e: e.reciprocal(sm[:, 0:64], sm[:, 0:64]), k)
        st = strip(w2[:, 2304:2816], 8, 512)
        zrel = [t_ss, t_ss]

        def ev_z(t, o, tok):
            z, q2 = zz_[t % 2], th2[t % 2]
            ka = act(lambda e: e.activation(q2, o, ACT.Tanh, scale=0.5), tok, zrel[t % 2], phase)
            k = dve(lambda e: e.scalar_tensor_tensor(out=z, in0=q2, scalar=1.0, in1=o, op0=ALU.add, op1=ALU.mult), ka,
                    zrel[t % 2])
            free_o = k
            k = dve(lambda e: e.tensor_tensor(v3(q2), v3(O[:, t, :]), bc(ss8[:, t, :].unsqueeze(2), [P, 8, 64]),
                                              ALU.mult), k, t_ss)
            k = dve(lambda e: e.tensor_tensor(q2, q2, dn, ALU.mult), k, t_dn)
            k = dve(lambda e: e.scalar_tensor_tensor(out=z, in0=z, scalar=0.5, in1=q2, op0=ALU.mult, op1=ALU.mult), k)
            b, free = banks.take()
            for j in range(4):
                tp = pe(lambda e, j=j: e.transpose(PS[b][:, j * 128:(j + 1) * 128], z[:, j * 128:(j + 1) * 128],
                                                   ident[:, :]), free, k)
            zrel[t % 2] = tp
            ke = act(lambda e: e.activation(yd[:, :, t * 128:(t + 1) * 128], hv(b), ACT.Copy), tp, phase)
            banks.give(b, ke)
            return free_o
        done(st, dense_tm(st, hlhs, range(8), 512, ev_z, t_h))
        t_yd = act.last()
        dump("yd", yd, t_yd)

        phase = everyone()
        MX = R3(F0 + 16384, 8, 1024)
        tmpx = Pool_([R(CB + i * 512, 512) for i in range(4)])
        slot, free = wring.take()
        wv = R3(W0 + slot * 4096, 4, 1024)
        sp.dma(wv[0:64, :, :], d["w_br_attn_2"][0:256, :].rearrange("(j f) n -> f j n", f=64), wsem[slot], free)
        tw = sp.dma(wv[64:128, :, :], d["w_br_attn_2"][256:512, :].rearrange("(j f) n -> f j n", f=64), wsem[slot])
        wa = (slot, wv, tw)
        sigmoid_mix(MX, None, 4, lambda k, n0, N: aq[:, k, n0:n0 + N],
                    lambda c: w2[:, 2848 + c * 512:3360 + c * 512], None, True, t_ya, tmpx, phase, att=wa)
        done(wa, pe.last())
        wa = strip(d["w_br_dn_2"], 4, 1024)
        k = sigmoid_mix(MX, None, 4, lambda k, n0, N: yd[:, k, n0:n0 + N],
                        lambda c: w2[:, 3872 + c * 512:4384 + c * 512], None, False, t_yd, tmpx, phase, att=wa)
        done(wa, pe.last())
        t_mx = [k, dve.last()]
        phase = everyone()
        dump("mix2", MX, t_mx)
        t_x = sp.dma(X, xs.rearrange("(t p) n -> p t n", p=P), stream("unstash"), phase, t_stash)

        def gate_row(c0, dst, tmp8, *toks):
            for h in range(2):
                b, free = banks.take()
                for q in range(4):
                    k = dve(lambda e, h=h, q=q: e.tensor_scalar(
                        tmp8[:, h * 4 + q, :], ident[:, :], mods[:, c0 + h * 4 + q:c0 + h * 4 + q + 1], None,
                        ALU.mult), *toks)
                tok = accumulate(PS[b][:, :], [(ones1, tmp8[:, h * 4:h * 4 + 4, :])], (free, k, t_one1))
                k = act(lambda e, b=b, h=h: e.activation(dst[:, h * 512:(h + 1) * 512], PS[b][:, :], ACT.Copy), tok,
                        *toks)
                banks.give(b, k)
            return k

        ones1 = R(52224, 128)
        t_one1 = gp(lambda e: e.memset(ones1, 1.0), phase)
        G1 = R(F1, 1024)
        t_g = gate_row(16, G1, R3(F1 + 1024, 8, 128), phase)
        tmpx = Pool_([R(CB + i * 512, 512) for i in range(4)])
        w_out_pass(d["w_out_2"], X, MX, t_mx, t_x, gate=(G1, t_g), tmp=tmpx)
        t_x = [gp.last(), t_x]
        dump("x2", X, t_x)

        phase = everyone()
        xn = Pool_([R3(F1, 4, 1024), R3(F1 + 4096, 4, 1024)])
        tk = norm_stats(Xt, 8, rs, R(F2, 1024), [t_x, phase])
        tmn = Pool_([TMP[:, i * 512:i * 512 + 512] for i in range(4)])
        t_h = norm_T3(Xt, rs, xn, lambda k: gs[:, 16 + k:17 + k], lambda k: mods[:, 24 + k:25 + k], (HH, HL), tmn,
                      [tk, phase], phase)
        phase = everyone()
        G2 = R(51200, 1024)
        t_g = gate_row(40, G2, R3(FF_F, 8, 128), phase)
        t_x = feed_forward(X, d["w_mlp1_2"], d["w_mlp2_2"], t_h, t_x, everyone(), gate=(G2, t_g))
        finish(nc, ctx, (pe, dve, act, gp, sp), out, X, t_x, dbg)

def finish(nc, ctx, queues, out, X, t_x, dbg):
    pe, dve, act, gp, sp = queues
    so = [ctx.enter_context(nc.semaphore("store")), 0]
    t = sp.dma(out.rearrange("(t p) n -> p t n", p=P), X, so, t_x)
    sp.wait(t, *[v[1] for v in dbg.values()])
    with nc.Block() as block:
        @block.sync
        def _(e):
            sp.replay(e)

        @block.tensor
        def _(e):
            pe.replay(e)

        @block.vector
        def _(e):
            dve.replay(e)

        @block.scalar
        def _(e):
            act.replay(e)

        @block.gpsimd
        def _(e):
            gp.replay(e)

DIRECT = ["x", "w_in", "w_att_o", "w_rg_a", "w_rg_i", "w_rec_o", "w_out", "w_ff1", "w_ff2", "ctx_2", "w_ada_2",
          "w_in_2", "w_br_attn_2", "w_br_dn_2", "w_out_2", "w_mlp1_2", "w_mlp2_2"]

def layout(inputs):
    a = {k: np.asarray(v) for k, v in inputs.items()}
    got = {n: np.ascontiguousarray(a[n].reshape(a[n].shape[1:])) for n in DIRECT}

    def col(v):
        return v.reshape(-1, 128).T

    b_in = a["b_in"][0]
    cols = {
        "ln1": col(a["ln1_g"][0]), "ln2": col(a["ln2_g"][0]), "bq": col(b_in[0:512]), "bk": col(b_in[512:1024]),
        "bu": col(b_in[1536:2560]), "by": col(b_in[2560:3584]), "bga": col(b_in[3584:4608]),
        "bgr": col(b_in[4608:5632]), "cw": col(a["conv_w"][0]), "cb": col(a["conv_b"][0]),
        "ba": col(a["b_rg_a"][0]), "bi": col(a["b_rg_i"][0]), "lam": col(a["lru_lambda"][0]),
        "c2": np.stack([col(a["c_2"][0]), col(a["c_ctx_2"])], 2).reshape(128, 16), "bada": col(a["b_ada_2"][0]),
        "g1": col(a["g_norm1_2"][0]), "g2": col(a["g_norm2_2"][0]), "cw2": col(a["conv_w_2"][0]),
    }
    got["vecs"] = np.ascontiguousarray(np.concatenate([cols[n] for n in VEC], 1))
    rows = {
        "bv": b_in[1024:1536], "lnf": a["lnf_g"],
        "qk": np.concatenate([np.tile(a["q_norm_g_2"][0], 8), np.tile(a["k_norm_g_2"][0], 2)]),
        "dn": np.tile(a["dn_norm_g_2"][0], 8), "dt": a["dt_bias_2"][0].reshape(-1), "al": a["a_log_2"][0].reshape(-1),
        "sink": a["attn_sink_2"][0],
    }
    row = np.concatenate([rows[n] for n in ROW])
    got["rows"] = np.ascontiguousarray(np.broadcast_to(row[None, :], (128, NROW)))
    q = np.arange(64)
    idx = np.clip(q[None, :] - q[:, None] + 15, 0, 30)
    nb = a["rpb"][0][:, :, idx]
    nb = nb.reshape(4, 2, 15, 64, 64).transpose(1, 3, 0, 2, 4)
    got["nbias"] = np.ascontiguousarray(nb.reshape(128, 4, 960))
    c = shape_constants()
    c["lv"] = c["lv"].reshape(128, 2, LEVELS, 128)
    c["cum"] = c["cum"].reshape(128, 2, 128)
    c["neg"] = c["neg"].reshape(128, 2, 128)
    c["rope"] = c["rope"].reshape(128, 8, 128)
    got.update(c)
    return got

def kernel(**inputs):
    import concourse.bacc as _bacc
    from concourse.bass_utils import run_bass_kernel_spmd as _run

    got = layout(inputs)
    nc = _bacc.Bacc("TRN2", target_bir_lowering=False, num_devices=1)
    arrays, d = {}, {}
    for name, v in got.items():
        arrays["in_" + name] = v
        d[name] = nc.dram_tensor("in_" + name, v.shape, mybir.dt.from_np(v.dtype), kind="ExternalInput").ap()
    d["w_ada"] = d["w_ada_2"]
    out = nc.dram_tensor("out_0", (S, 1024), F32, kind="ExternalOutput").ap()
    build(nc, d, out)
    r = _run(nc, [arrays], core_ids=[0])
    return r.results[0]["out_0"].reshape(1, S, 1024)
```
